# Optimizing a Trainium2 kernel written in Bass

```python
import jax, jax.numpy as jnp
from jax import lax
import numpy as np

D_MODEL = 2048
BATCH = 1
SEQ = 256
DEPTH = 1
DEC_BATCH = 8
DEC_SEQ = 1
PAST_LEN = 2048
PAGE_SIZE = 128

D_POOL = D_MODEL // 2
POOL_WINDOWS = (2, 4, 8, 16)
POOL_GROUPS = len(POOL_WINDOWS)
POOL_GROUP_DIM = D_POOL // POOL_GROUPS
POOL_BUF = max(POOL_WINDOWS) - 1
N_HEADS = 8
HEAD_DK = D_MODEL // 16
HEAD_DV = D_MODEL // 8
D_QK = N_HEADS * HEAD_DK
D_V = N_HEADS * HEAD_DV
CHUNK = 128
ROPE_BASE = 10000.0
EPS = 1e-6
D_IN = 2 * D_POOL + 2 * D_QK + 2 * D_V
SPLITS = (D_POOL, 2 * D_POOL, 2 * D_POOL + D_QK, 2 * D_POOL + 2 * D_QK, 2 * D_POOL + 2 * D_QK + D_V)

kernel_name = 'pool_retention_gated_hybrid_step'

def rmsnorm(x, g):
    xf = x.astype(jnp.float32)
    xf = xf * lax.rsqrt(jnp.mean(xf * xf, axis=-1, keepdims=True) + EPS)
    return xf * g.astype(jnp.float32)

def rotary(x, start):
    T = x.shape[1]
    half = HEAD_DK // 2
    inv = ROPE_BASE ** (-jnp.arange(half, dtype=jnp.float32) / half)
    pos = start + jnp.arange(T, dtype=jnp.float32)
    ang = pos[:, None] * inv[None, :]
    cos = jnp.cos(ang)[None, :, None, :]
    sin = jnp.sin(ang)[None, :, None, :]
    x1, x2 = x[..., :half], x[..., half:]
    return jnp.concatenate([x1 * cos - x2 * sin, x1 * sin + x2 * cos], axis=-1)

def pool_mixer(xa, buf, start, pool_w, pool_scale):
    B, T, _ = xa.shape
    P = POOL_BUF
    ext = jnp.concatenate([buf.astype(jnp.float32), xa.astype(jnp.float32)], axis=1)
    cs = jnp.concatenate([jnp.zeros((B, 1, D_POOL), jnp.float32), jnp.cumsum(ext, axis=1)], axis=1)
    pos = start + jnp.arange(T)
    outs = []
    for g, w in enumerate(POOL_WINDOWS):
        sl = slice(g * POOL_GROUP_DIM, (g + 1) * POOL_GROUP_DIM)
        win = cs[:, P + 1:P + 1 + T, sl] - cs[:, P + 1 - w:P + 1 - w + T, sl]
        cnt = jnp.minimum(pos + 1, w).astype(jnp.float32)[None, :, None]
        outs.append(win / cnt - ext[:, P:, sl])
    pooled = jnp.stack(outs, axis=2)
    mixed = jnp.einsum('btgc,gcd->btgd', pooled, pool_w).reshape(B, T, D_POOL) * pool_scale
    return mixed, ext[:, -POOL_BUF:]

def retention(q, k, v, S0):
    B, H, T, _ = q.shape
    C = min(CHUNK, T)
    NC = T // C
    lg = jnp.log1p(-jnp.power(2.0, -5.0 - jnp.arange(N_HEADS, dtype=jnp.float32)))
    idx = jnp.arange(C, dtype=jnp.float32)
    diff = idx[:, None] - idx[None, :]
    dmask = jnp.where(diff[None] >= 0, jnp.exp(jnp.maximum(diff, 0.0)[None] * lg[:, None, None]), 0.0)
    q_dec = jnp.exp((idx + 1.0)[None, :] * lg[:, None])[..., None]
    k_dec = jnp.exp((C - 1.0 - idx)[None, :] * lg[:, None])[..., None]
    chunk_dec = jnp.exp(C * lg)[:, None, None]

    def to_chunks(a):
        return jnp.moveaxis(a.reshape(B, H, NC, C, a.shape[-1]), 2, 0)

    def step(S, inp):
        qc, kc, vc = inp
        scores = jnp.einsum('bhld,bhmd->bhlm', qc, kc) * dmask
        o = jnp.einsum('bhlm,bhmv->bhlv', scores, vc) + jnp.einsum('bhld,bhdv->bhlv', qc * q_dec, S)
        S = chunk_dec * S + jnp.einsum('bhld,bhlv->bhdv', kc * k_dec, vc)
        return S, o

    S, o = lax.scan(step, S0, (to_chunks(q), to_chunks(k), to_chunks(v)))
    o = jnp.moveaxis(o, 0, 2).reshape(B, H, T, HEAD_DV)
    return o, S

def mixer_layer(x, c, buf, S0, start, ada_w, ada_b, g_pre, g_post, w_in, pool_w, pool_scale,
                gn_g, w_a_proj, w_b_proj, w_merge, b_merge, w_out):
    B, T, _ = x.shape
    mod = jax.nn.silu(c.astype(jnp.float32)) @ ada_w + ada_b
    shift, scale, gate = jnp.split(mod, 3, axis=-1)
    h = rmsnorm(x, g_pre) * (1.0 + scale[:, None]) + shift[:, None]
    z = h @ w_in
    a_x, a_g, q, k, v, b_g = jnp.split(z, SPLITS, axis=-1)
    y_a, new_buf = pool_mixer(a_x, buf, start, pool_w, pool_scale)
    y_a = y_a * jax.nn.silu(a_g)
    q = rotary(q.reshape(B, T, N_HEADS, HEAD_DK), start)
    k = rotary(k.reshape(B, T, N_HEADS, HEAD_DK), start) * (HEAD_DK ** -0.5)
    v = v.reshape(B, T, N_HEADS, HEAD_DV)
    o, S = retention(q.transpose(0, 2, 1, 3), k.transpose(0, 2, 1, 3), v.transpose(0, 2, 1, 3),
                     S0.astype(jnp.float32))
    o = o.transpose(0, 2, 1, 3)
    mu = jnp.mean(o, axis=-1, keepdims=True)
    var = jnp.mean(jnp.square(o - mu), axis=-1, keepdims=True)
    o = (o - mu) * lax.rsqrt(var + EPS) * gn_g
    y_b = o.reshape(B, T, D_V) * jax.nn.silu(b_g)
    ya = y_a @ w_a_proj
    yb = y_b @ w_b_proj
    gates = jax.nn.sigmoid(h @ w_merge + b_merge)
    g_a, g_b = jnp.split(gates, 2, axis=-1)
    out = rmsnorm((g_a * ya + g_b * yb) @ w_out, g_post)
    y = x.astype(jnp.float32) + gate[:, None] * out
    return y.astype(x.dtype), new_buf.astype(buf.dtype), S.astype(S0.dtype)

def setup_inputs(seed: int = 0) -> dict:
    key = jax.random.key(seed)
    ks = jax.random.split(key, 20)
    f32 = jnp.float32
    nrm = lambda k, shape, s: jax.random.normal(k, shape, f32) * s
    D = D_MODEL
    return {
        'x_prompt': nrm(ks[0], (BATCH, SEQ, D), 1.0),
        'x_sample': nrm(ks[1], (DEC_BATCH, DEC_SEQ, D), 1.0),
        'state_pool': nrm(ks[2], (DEPTH, DEC_BATCH, POOL_BUF, D_POOL), 1.0),
        'state_ret': nrm(ks[3], (DEPTH, DEC_BATCH, N_HEADS, HEAD_DK, HEAD_DV), 0.5),
        'c_prompt': nrm(ks[4], (BATCH, D), 1.0),
        'c_sample': nrm(ks[5], (DEC_BATCH, D), 1.0),
        'ada_w': nrm(ks[6], (DEPTH, D, 3 * D), 0.5 * D ** -0.5),
        'ada_b': nrm(ks[7], (DEPTH, 3 * D), 0.02),
        'g_pre': 1.0 + nrm(ks[8], (DEPTH, D), 0.02),
        'g_post': 1.0 + nrm(ks[9], (DEPTH, D), 0.02),
        'w_in': nrm(ks[10], (DEPTH, D, D_IN), D ** -0.5),
        'pool_w': nrm(ks[11], (DEPTH, POOL_GROUPS, POOL_GROUP_DIM, POOL_GROUP_DIM), POOL_GROUP_DIM ** -0.5),
        'pool_scale': 1.0 + nrm(ks[12], (DEPTH, D_POOL), 0.02),
        'gn_g': 1.0 + nrm(ks[13], (DEPTH, N_HEADS, HEAD_DV), 0.02),
        'w_a_proj': nrm(ks[14], (DEPTH, D_POOL, D), D_POOL ** -0.5),
        'w_b_proj': nrm(ks[15], (DEPTH, D_V, D), D_V ** -0.5),
        'w_merge': nrm(ks[16], (DEPTH, D, 2 * D), D ** -0.5),
        'b_merge': nrm(ks[17], (DEPTH, 2 * D), 0.02),
        'w_out': nrm(ks[18], (DEPTH, D, D), D ** -0.5),
    }

def reference(x_prompt, x_sample, state_pool, state_ret, c_prompt, c_sample, ada_w, ada_b, g_pre, g_post,
              w_in, pool_w, pool_scale, gn_g, w_a_proj, w_b_proj, w_merge, b_merge, w_out):
    xp, xs = x_prompt, x_sample
    pool_p, ret_p, pool_s, ret_s = [], [], [], []
    for l in range(DEPTH):
        params = (ada_w[l], ada_b[l], g_pre[l], g_post[l], w_in[l], pool_w[l], pool_scale[l], gn_g[l],
                  w_a_proj[l], w_b_proj[l], w_merge[l], b_merge[l], w_out[l])
        buf0 = jnp.zeros((xp.shape[0], POOL_BUF, D_POOL), state_pool.dtype)
        S00 = jnp.zeros((xp.shape[0], N_HEADS, HEAD_DK, HEAD_DV), state_ret.dtype)
        xp, bp, sp = mixer_layer(xp, c_prompt, buf0, S00, 0, *params)
        xs, bs, ss = mixer_layer(xs, c_sample, state_pool[l], state_ret[l], PAST_LEN, *params)
        pool_p.append(bp)
        ret_p.append(sp)
        pool_s.append(bs)
        ret_s.append(ss)
    new_pool_prompt = jnp.stack(pool_p, axis=0)
    new_ret_prompt = jnp.stack(ret_p, axis=0)
    new_pool_sample = jnp.stack(pool_s, axis=0)
    new_ret_sample = jnp.stack(ret_s, axis=0)
    return (xp, xs, new_pool_prompt, new_ret_prompt, new_pool_sample, new_ret_sample)


_drawn_inputs = setup_inputs


def setup_inputs(seed=0):
    import zlib

    import numpy as np

    out = dict(_drawn_inputs(seed))
    spreads = {}
    factors = {'g_post': 8.0, 'pool_scale': 8.0, 'gn_g': 8.0, 'b_merge': 8.0}
    for name, (base, spread) in spreads.items():
        noise = np.random.default_rng([zlib.crc32(name.encode()), seed]).standard_normal(out[name].shape)
        drawn = base * np.exp(spread * noise) if base else spread * noise
        out[name] = __import__('jax').numpy.asarray(drawn.astype(out[name].dtype))
    for name, factor in factors.items():
        out[name] = (out[name] * factor).astype(out[name].dtype)
    return out
```

```python
import numpy as np
import concourse.bass as bass
from concourse import mybir
from contextlib import ExitStack

D_MODEL = 2048
TP = 256
TS = 8
NT = TP + TS
KT = D_MODEL // 128
NC = 1 + TS
D_POOL = D_MODEL // 2
WINDOWS = (2, 4, 8, 16)
POOL_BUF = max(WINDOWS) - 1
H = 8
DK = D_MODEL // 16
DV = D_MODEL // 8
PAST_LEN = 2048
EPS = 1e-6
UNIT = KT * 128
AW = 256
V_GPRE, V_GPOST, V_ADAB, V_BMERGE, V_PSCALE = 0, 16, 32, 80, 112
V_N = 120
HC_KD0, HC_KD1, HC_GAMMA, HC_GN = TP, TP + 1, TP + 2, TP + 3
HC_N = TP + 5


def outs(a, c, after_ya=False):
    i = 6 * a + c
    if not isinstance(a, int):
        return i + (9 if after_ya else 1)
    return i + 1 if i < 64 else (64 + 2 * (i - 63) if i < 72 else i + 9)


def build(nc, stream, ada0, ada1, xT, cT, vec, headc, trig, ident_in, sel_in, cnt_in, poolw, spool,
          sret, yT, npool_p, npool_s, nret_p, nret_s):
    f32, f32r = mybir.dt.float32, mybir.dt.float32r
    ALU, ACT, AX = mybir.AluOpType, mybir.ActivationFunctionType, mybir.AxisListType

    ctx = ExitStack()
    with ctx:
        def sb(name, shape, dt=f32, stack=ctx):
            return stack.enter_context(nc.sbuf_tensor(name, shape, dt))

        def sem(name):
            return ctx.enter_context(nc.semaphore(name))

        raw = sb("raw", [128, 3, UNIT])
        w_hi = sb("w_hi", [128, 3, UNIT], f32r)
        w_lo = sb("w_lo", [128, 2, UNIT], f32r)
        h_hi = sb("h_hi", [128, KT, NT], f32r)
        h_lo = sb("h_lo", [128, KT, NT], f32r)
        cpad = sb("cpad", [128, KT, 32])
        c_in = sb("c_in", [128, KT, NC])
        part = sb("part", [128, 2, AW])
        vecs = sb("vecs", [128, V_N])
        ident = sb("ident", [128, 128])
        ones = sb("ones", [128, 128])
        sel = sb("sel", [128, NC])
        eps_t = sb("eps_t", [128, 1])
        mod_scale = sb("mod_scale", [128, 2, NC])
        mod_shift = sb("mod_shift", [128, 2, NC])
        gate_g = sb("gate_g", [128, KT, NC])
        early = ExitStack()
        ada_ring = sb("ada_ring", [128, 4, UNIT], f32, early)
        x_t = sb("x_t", [128, KT, NT], f32, early)
        early.close()
        yb_hi = sb("yb_hi", [128, KT, NT], f32r)
        yb_lo = sb("yb_lo", [128, KT, NT], f32r)
        mid = ExitStack()
        ya_hi = sb("ya_hi", [128, KT // 2, NT], f32r, mid)
        ya_lo = sb("ya_lo", [128, KT // 2, NT], f32r, mid)
        work = sb("work", [128, 4, 16 + TP], f32, mid)
        qk_t = sb("qk_t", [128, 2, NT], f32, mid)
        v_t = sb("v_t", [128, 2, NT], f32, mid)
        scm = sb("scm", [128, 512], f32, mid)
        v_nat = sb("v_nat", [128, 512], f32, mid)
        kd = sb("kd", [128, 2, 128], f32, mid)
        diag_hi = sb("diag_hi", [128, 4, 2, 128], f32r, mid)
        diag_lo = sb("diag_lo", [128, 4, 2, 128], f32r, mid)
        vs_hi = sb("vs_hi", [128, 2, TS], f32r, mid)
        vs_lo = sb("vs_lo", [128, 2, TS], f32r, mid)
        ones_r = sb("ones_r", [128, 128], f32r, mid)
        s_t = sb("s_t", [128, TS, DV], f32, mid)
        sp_t = sb("sp_t", [128, DV], f32, mid)
        o_t = sb("o_t", [128, 2, NT], f32, mid)
        sq_t = sb("sq_t", [128, 2, NT], f32, mid)
        osum = sb("osum", [128, NT], f32, mid)
        rstd = sb("rstd", [128, NT], f32, mid)
        bg_t = sb("bg_t", [128, 2, NT], f32, mid)
        qpad = sb("qpad", [128, TS, 32], f32, mid)
        trig_t = sb("trig_t", [128, 2, NT], f32, mid)
        hc = sb("hc", [128, HC_N], f32, mid)
        gn_cur = sb("gn_cur", [128, 2], f32, mid)
        ext = sb("ext", [128, 2, 16 + TP], f32, mid)
        exts = sb("exts", [128, 2, TS, 16], f32, mid)
        sp_in = sb("sp_in", [128, 2, TS, POOL_BUF], f32, mid)
        nps_t = sb("nps_t", [128, 2, TS, POOL_BUF], f32, mid)
        npp_t = sb("npp_t", [128, 8, POOL_BUF], f32, mid)
        cnt_t = sb("cnt_t", [128, 4, 16], f32, mid)
        win_s = sb("win_s", [128, 2, TS], f32, mid)
        mid.close()
        late = ExitStack()
        m_hi = sb("m_hi", [128, KT, NT], f32r, late)
        ya_out = sb("ya_out", [128, KT, NT], f32, late)
        m_lo = sb("m_lo", [128, KT, NT], f32r, late)
        gate_ring = sb("gate_ring", [128, 2, UNIT], f32, late)
        sig_a = sb("sig_a", [128, NT], f32, late)
        sig_b = sb("sig_b", [128, NT], f32, late)
        yb_out = sb("yb_out", [128, NT], f32, late)
        m_f = sb("m_f", [128, NT], f32, late)
        late.close()
        h_f = v_t
        q_raw, q_swap, q_cos = work[:, 0, 0:NT], work[:, 1, 0:NT], work[:, 2, 0:NT]
        pooled, pool_w, sil_a, ya_f = v_t, v_nat, qk_t, trig_t

        banks = [ctx.enter_context(nc.psum_tensor(f"bank{n}", [128, 512], f32)) for n in range(8)]
        P = banks[0:2]
        TR, TV, SC, O0, O1, ST = banks[2:8]

        const_in = sem("const_in")
        x_in = sem("x_in")
        trig_in = sem("trig_in")
        raw_loaded = [sem(f"raw_loaded{s}") for s in range(3)]
        hi_ready, lo_ready = sem("hi_ready"), sem("lo_ready")
        proj_done, taken = sem("proj_done"), sem("taken")
        ada_loaded = [sem(f"ada_loaded{s}") for s in range(4)]
        ada_used, part_ready, sel_done = sem("ada_used"), sem("part_ready"), sem("sel_done")
        mod_ready, hf_ready, h_hi_ready, h_lo_ready = sem("mod_ready"), sem("hf_ready"), sem("h_hi_ready"), sem("h_lo_ready")
        c_zero, c_ready, const_ready = sem("c_zero"), sem("c_ready"), sem("const_ready")
        x_sq, x_sum, x_ms, x_std, x_rstd, xn_ready = (sem("x_sq"), sem("x_sum"), sem("x_ms"), sem("x_std"),
                                                      sem("x_rstd"), sem("xn_ready"))
        hs_mul = sem("hs_mul")
        head_in, state_in, state_out, sp_out = sem("head_in"), sem("state_in"), sem("state_out"), sem("sp_out")
        qk_evac, rot_mul, rotated, qpad_ready = sem("qk_evac"), sem("rot_mul"), sem("rotated"), sem("qpad_ready")
        v_ready, vs_hi_ready, vs_lo_ready, diag_ready = sem("v_ready"), sem("vs_hi_ready"), sem("vs_lo_ready"), sem("diag_ready")
        bg_ready = sem("bg_ready")
        step_a, step_b, step_c0, step_c1, step_d, step_e, step_f = (sem(f"step_{x}") for x in ("a", "b", "c0", "c1", "d", "e", "f"))
        vnat_ready, kd_ready, scm_ready = sem("vnat_ready"), sem("kd_ready"), sem("scm_ready")
        o_ready, sp_ready, s_scaled, s_new, os_ready = sem("o_ready"), sem("sp_ready"), sem("s_scaled"), sem("s_new"), sem("os_ready")
        o_samples, osum_ready, cen_ready, sq_ready, sqs_ready = (sem("o_samples"), sem("osum_ready"), sem("cen_ready"),
                                                                 sem("sq_ready"), sem("sqs_ready"))
        std_ready, rstd_ready, ynorm_ready, yf_ready, yhi_ready, ylo_ready, gn_saved = (
            sem("std_ready"), sem("rstd_ready"), sem("ynorm_ready"), sem("yf_ready"), sem("yhi_ready"), sem("ylo_ready"), sem("gn_saved"))
        spool_in, poolw_in, spool_out = sem("spool_in"), sem("poolw_in"), sem("spool_out")
        ax_evac, exts_old, win_ready, win_step, wins_ready = sem("ax_evac"), sem("exts_old"), sem("win_ready"), sem("win_step"), sem("wins_ready")
        head_cols, pooled_ready, sag_ready, pool_mm = sem("head_cols"), sem("pooled_ready"), sem("sag_ready"), sem("pool_mm")
        yaf_ready, yahi_ready, yalo_ready, npool_ready, ppool_ready, ppool_out = (
            sem("yaf_ready"), sem("yahi_ready"), sem("yalo_ready"), sem("npool_ready"), sem("ppool_ready"), sem("ppool_out"))
        gate_loaded = [sem(f"gate_loaded{s}") for s in range(2)]
        gate_used, gpart_ready, gsel_done, gbias_ready, gate_ready = (
            sem("gate_used"), sem("gpart_ready"), sem("gsel_done"), sem("gbias_ready"), sem("gate_ready"))
        branch_ready, merge_mul, mf_ready, mhi_ready, mlo_ready = (
            sem("branch_ready"), sem("merge_mul"), sem("mf_ready"), sem("mhi_ready"), sem("mlo_ready"))
        out_evac, out_sq, out_acc, out_gated, out_ms, out_std, out_rstd = (
            sem("out_evac"), sem("out_sq"), sem("out_acc"), sem("out_gated"), sem("out_ms"), sem("out_std"), sem("out_rstd"))
        x_again, y_scaled, y_ready, y_out = sem("x_again"), sem("y_scaled"), sem("y_ready"), sem("y_out")
        y_scaled_p, y_ready_p = sem("y_scaled_p"), sem("y_ready_p")
        x_late = raw[:, :, :].rearrange("p s n -> p (s n)")[:, 0:KT * NT].rearrange("p (k t) -> p k t", k=KT)

        block = ctx.enter_context(nc.Block())

        @block.sync
        def _(sp):
            def load(a, c):
                i = 6 * a + c
                if not isinstance(a, int) or i >= 3:
                    sp.wait_ge(lo_ready, i - 2)
                sp.dma_start(raw[:, c % 3, :], stream[i]).then_inc(raw_loaded[c % 3], 16)

            sp.dma_start(c_in[:, :, :], cT).then_inc(const_in, 16)
            sp.dma_start(vecs[:, :], vec).then_inc(const_in, 16)
            sp.dma_start(ident[:, :], ident_in).then_inc(const_in, 16)
            sp.dma_start(sel[:, :], sel_in).then_inc(const_in, 16)
            sp.dma_start(x_t[:, :, :], xT).then_inc(x_in, 16)
            for s in range(4):
                sp.dma_start(ada_ring[:, s, :], ada0[s]).then_inc(ada_loaded[s], 16)
            load(0, 0)
            sp.dma_start(trig_t[:, :, :], trig).then_inc(trig_in, 16)
            sp.dma_start(cnt_t[:, :, :], cnt_in).then_inc(trig_in, 16)
            sp.dma_start(hc[:, :], headc[0]).then_inc(head_in, 16)
            with sp.Fori(1, 8) as p:
                for s in range(4):
                    sp.wait_ge(ada_used, 4 * p + s - 3)
                    sp.dma_start(ada_ring[:, s, :], ada0[4 * p + s]).then_inc(ada_loaded[s], 16)
            load(0, 1)
            load(0, 2)
            sp.dma_start(s_t[:, :, :], sret[0]).then_inc(state_in, 16)
            for c in range(3, 9):
                load(0, c)

            def head_stores(g):
                sp.wait_ge(sp_ready, g + 1)
                sp.dma_start(nret_p[g], sp_t[:, :]).then_inc(sp_out, 16)
                sp.wait_ge(s_new, 4 * g + 4)
                sp.dma_start(nret_s[g], s_t[:, :, :]).then_inc(state_out, 16)

            with sp.Fori(1, H) as h:
                for c in range(6):
                    if c == 2:
                        sp.wait_ge(gn_saved, h)
                        sp.wait_ge(s_scaled, h)
                        sp.dma_start(hc[:, :], headc[h]).then_inc(head_in, 16)
                    if c == 4:
                        head_stores(h - 1)
                    if c == 5:
                        sp.wait_ge(state_out, 16 * h)
                        sp.wait_ge(step_c1, h)
                        sp.dma_start(s_t[:, :, :], sret[h]).then_inc(state_in, 16)
                    load(h, c + 3)
            for i in range(51, 75):
                g, r = divmod(i - 51, 4)
                if g < 4 and r == 0:
                    if g >= 1:
                        sp.wait_ge(exts_old, g)
                    sp.dma_start(sp_in[:, :, :, :], spool[g]).then_inc(spool_in, 16)
                    if g == 0:
                        sp.wait_ge(step_b, H)
                    else:
                        sp.wait_ge(pool_mm, g)
                    sp.dma_start(pool_w[:, :], poolw[g]).then_inc(poolw_in, 16)
                if i == 52:
                    head_stores(H - 1)
                if r == 3 and g < 4:
                    sp.wait_ge(npool_ready, g + 1)
                    sp.dma_start(npool_s[g], nps_t[:, :, :, :]).then_inc(spool_out, 16)
                if i == 67:
                    sp.wait_ge(ppool_ready, 4)
                    sp.dma_start(npool_p, npp_t[:, :, :]).then_inc(ppool_out, 16)
                load(8, i - 48)
            sp.wait_ge(ylo_ready, H)
            sp.wait_ge(yalo_ready, 4)
            sp.wait_ge(state_out, 16 * H)
            sp.wait_ge(sp_out, 16 * H)
            sp.wait_ge(spool_out, 64)
            sp.wait_ge(ppool_out, 16)
            for s in range(2):
                sp.dma_start(gate_ring[:, s, :], ada1[s]).then_inc(gate_loaded[s], 16)
            with sp.Fori(0, 7) as it:
                for c in range(6):
                    load(12 + it, c + 3)
                    if c in (4, 5):
                        s = c - 4
                        sp.wait_ge(gate_used, 2 * it + s + 1)
                        sp.dma_start(gate_ring[:, s, :], ada1[2 * it + 2 + s]).then_inc(gate_loaded[s], 16)
            for c in range(6):
                load(19, c + 3)
            for i in range(123, 136):
                load(20, i - 120)
            sp.wait_ge(lo_ready, 136)
            sp.dma_start(x_late, xT).then_inc(x_again, 16)
            for q in range(3):
                sp.wait_ge(y_ready, q + 1)
                sp.dma_start(yT[:, 4 * q:4 * q + 4, :], ya_out[:, 4 * q:4 * q + 4, :]).then_inc(y_out, 16)
            sp.wait_ge(y_ready_p, 1)
            sp.dma_start(yT[:, 12:16, :], ya_out[:, 12:16, :]).then_inc(y_out, 16)
            sp.wait_ge(y_out, 64)

        @block.tensor
        def _(pe):
            def ada_unit(bank, w, half):
                for k in range(8):
                    j = k % 4
                    mm = pe.matmul(bank[32 * j:32 * j + 32, 0:AW], cpad[:, 8 * half + k, :],
                                   w[:, AW * k:AW * k + AW], start=(half == 0 and k < 4),
                                   stop=(half == 1 and k >= 4), tile_position=(0, 32 * j))
                return mm

            def select(bank, kind):
                for t in range(2):
                    col = (2 * kind + t) * 16
                    mm = pe.matmul(bank[:, col:col + NC], part[:, kind, 128 * t:128 * t + 128], sel[:, :],
                                   start=True, stop=True)
                return mm

            def project(a, c, hi, lo, depth=KT, parts=1, after_ya=False):
                i = 6 * a + c
                pe.wait_ge(lo_ready, i + 1)
                first = outs(a, c, after_ya) - parts
                for m in range(parts):
                    par = (c + m) % 2 if parts == 1 else m % 2
                    if not isinstance(a, int) or first + m >= 2:
                        pe.wait_ge(taken, first + m - 1)
                    out = P[par][:, 0:NT]
                    for k in range(depth):
                        col = (m * depth + k) * 128
                        wh, wl = w_hi[:, c % 3, col:col + 128], w_lo[:, c % 2, col:col + 128]
                        pe.matmul(out, wh, hi[:, k, :], start=(k == 0), stop=False)
                        pe.matmul(out, wh, lo[:, k, :], start=False, stop=False)
                        mm = pe.matmul(out, wl, hi[:, k, :], start=False, stop=(k == depth - 1))
                    mm.then_inc(proj_done, 1)

            pe.wait_ge(const_in, 64)
            pe.wait_ge(c_ready, 1)
            pe.wait_ge(const_ready, 1)

            def ada_pair(p):
                for s in range(4):
                    kind, half = divmod(s, 2)
                    pe.wait_ge(ada_loaded[s], 16 * p + 16)
                    if half == 0 and not (isinstance(p, int) and p == 0):
                        pe.wait_ge(part_ready, 2 * p - 1 + kind)
                    ada_unit((TR, TV)[kind], ada_ring[:, s, :], half).then_inc(ada_used, 1)
                if not (isinstance(p, int) and p == 0):
                    pe.wait_ge(mod_ready, 2 * p)
                for kind in range(2):
                    pe.wait_ge(part_ready, 2 * p + 1 + kind)
                    select(SC, kind).then_inc(sel_done, 1)

            ada_pair(0)
            pe.wait_ge(x_sum, KT // 2)
            pe.matmul(O0[:, 0:NT], ones[:, :], osum[:, :], start=True, stop=True).then_inc(x_ms, 1)
            with pe.Fori(1, 8) as p:
                ada_pair(p)

            def a_step(h):
                pe.wait_ge(rotated, 2 * h + 2)
                pe.wait_ge(v_ready, 2 * h + 2)
                if not (isinstance(h, int) and h == 0):
                    pe.wait_ge(s_new, 4 * h)
                    pe.wait_ge(cen_ready, 2 * h)
                q, k = qk_t[:, 0, :], qk_t[:, 1, :]
                for c in range(2):
                    pe.transpose(TR[:, 128 * c:128 * c + 128], k[:, 128 * c:128 * c + 128], ident[:, :])
                for c in range(2):
                    for t in range(2):
                        pe.transpose(TV[:, 256 * c + 128 * t:256 * c + 128 * t + 128],
                                     v_t[:, t, 128 * c:128 * c + 128], ident[:, :])
                pe.matmul(SC[:, 0:256], k[:, 0:128], q[:, 0:256], start=True, stop=True)
                pe.matmul(SC[:, 256:384], k[:, 128:256], q[:, 128:256], start=True, stop=True).then_inc(step_a, 1)

            def spread_v(n, bank):
                m = n % 2
                dh = diag_hi[:, 2 * m:2 * m + 2, :, :].rearrange("p b t n -> p (b t n)")
                dl = diag_lo[:, 2 * m:2 * m + 2, :, :].rearrange("p b t n -> p (b t n)")
                pe.matmul(bank[:, :], ones_r[:, :], dh, start=True, stop=False)
                return pe.matmul(bank[:, :], ones_r[:, :], dl, start=False, stop=True)

            def b_step(h):
                pe.wait_ge(vnat_ready, h + 1)
                pe.wait_ge(scm_ready, 2 * h + 2)
                if not (isinstance(h, int) and h == 0):
                    pe.wait_ge(std_ready, h)
                    pe.wait_ge(o_ready, 2 * h)
                for t, bank in enumerate((O0, O1)):
                    pe.matmul(bank[:, 0:256], v_nat[:, 128 * t:128 * t + 128], scm[:, 0:256], start=True, stop=False)
                    mm = pe.matmul(bank[:, 128:256], v_nat[:, 256 + 128 * t:384 + 128 * t], scm[:, 256:384],
                                   start=False, stop=True)
                pe.wait_ge(kd_ready, 2 * h + 2)
                if not (isinstance(h, int) and h == 0):
                    pe.wait_ge(o_samples, h)
                pe.matmul(ST[:, 0:256], kd[:, 0, :], v_nat[:, 0:256], start=True, stop=False)
                pe.matmul(ST[:, 0:256], kd[:, 1, :], v_nat[:, 256:512], start=False, stop=True)
                pe.wait_ge(diag_ready, 4 * h + 2)
                spread_v(0, TR)
                spread_v(1, TV).then_inc(step_b, 1)

            def c0_step(g):
                pe.wait_ge(diag_ready, 4 * g + 4)
                pe.wait_ge(s_new, 4 * g + 2)
                spread_v(2, TR)
                spread_v(3, TV).then_inc(step_c0, 1)

            def c1_step(g):
                pe.wait_ge(s_new, 4 * g + 4)
                pe.wait_ge(qpad_ready, g + 1)
                for b in range(TS):
                    j, i = b % 4, b // 4
                    mm = pe.matmul(SC[32 * j:32 * j + 32, 256 * i:256 * i + 256], qpad[:, b, :], s_t[:, b, :],
                                   start=True, stop=True, tile_position=(0, 32 * j))
                mm.then_inc(step_c1, 1)

            def d_step(g):
                pe.wait_ge(os_ready, g + 1)
                pe.wait_ge(sp_ready, g + 1)
                for n in range(4):
                    mm = pe.transpose(ST[:, 128 * n:128 * n + 128], scm[:, 128 * n:128 * n + 128], ident[:, :])
                mm.then_inc(step_d, 1)

            def e_step(g):
                pe.wait_ge(osum_ready, g + 1)
                pe.matmul(SC[:, 0:NT], ones[:, :], osum[:, :], start=True, stop=True).then_inc(step_e, 1)

            def f_step(g):
                pe.wait_ge(sqs_ready, g + 1)
                pe.matmul(O0[:, 0:NT], ones[:, :], osum[:, :], start=True, stop=True).then_inc(step_f, 1)

            def head(h, first=False):
                for c in range(6):
                    project(h, c, h_hi, h_lo)
                    if not first:
                        (c0_step, c1_step, d_step, e_step, f_step, lambda g: None)[c](h - 1)
                    if c == 4:
                        a_step(h)
                    if c == 5:
                        b_step(h)

            pe.wait_ge(h_lo_ready, 8)
            pe.wait_ge(const_ready, 2)
            head(0, first=True)
            with pe.Fori(1, H) as h:
                head(h)

            for g in range(4):
                for r in range(4):
                    project(8, 4 * g + r, h_hi, h_lo)
                    if g == 0:
                        (c0_step, c1_step, d_step, e_step)[r](H - 1)
                    if g == 1 and r == 0:
                        f_step(H - 1)
                pe.wait_ge(pooled_ready, 3 * g + 3)
                pe.wait_ge(poolw_in, 16 * g + 16)
                if g >= 1:
                    pe.wait_ge(yaf_ready, 2 * g)
                for t, bank in enumerate((O1, TR)):
                    for k in range(2):
                        mm = pe.matmul(bank[:, 0:NT], pool_w[:, 256 * k + 128 * t:256 * k + 128 * t + 128],
                                       pooled[:, k, :], start=(k == 0), stop=(k == 1))
                mm.then_inc(pool_mm, 1)

            pe.wait_ge(yalo_ready, 4)
            for u in range(8):
                project(8, 16 + u, ya_hi, ya_lo, depth=8, parts=2)

            pe.wait_ge(ylo_ready, H)
            pe.wait_ge(yaf_ready, 8)

            def merge(it, first=False):
                a = 12 + it
                for c in range(6):
                    if c % 3 < 2:
                        project(a, c, h_hi, h_lo, after_ya=True)
                    else:
                        project(a, c, yb_hi, yb_lo, after_ya=True)
                    if c in (1, 3):
                        s = (c - 1) // 2
                        pe.wait_ge(gate_loaded[s], 16 * it + 16)
                        if s == 0 and not first:
                            pe.wait_ge(gpart_ready, it)
                        ada_unit(TR, gate_ring[:, s, :], s).then_inc(gate_used, 1)
                    if c == 5:
                        pe.wait_ge(gpart_ready, it + 1)
                        if not first:
                            pe.wait_ge(gbias_ready, it)
                        select(SC, 0).then_inc(gsel_done, 1)

            merge(0, first=True)
            with pe.Fori(1, 8) as it:
                merge(it)

            pe.wait_ge(mlo_ready, KT)
            with pe.Fori(0, 2) as n:
                for c in range(6):
                    project(20 + n, c, m_hi, m_lo, after_ya=True)
            for c in range(4):
                project(22, c, m_hi, m_lo)
            pe.wait_ge(out_acc, KT)
            pe.matmul(O0[:, 0:NT], ones[:, :], sig_b[:, :], start=True, stop=True).then_inc(out_ms, 1)

        @block.scalar
        def _(act):
            def split(a, c, after_ya=False):
                i = 6 * a + c
                act.wait_ge(raw_loaded[c % 3], 16 * (2 * a + c // 3) + 16)
                if not isinstance(a, int):
                    act.wait_ge(proj_done, outs(a, c - 3, after_ya))
                elif i >= 3:
                    act.wait_ge(proj_done, outs(0, i - 3))
                act.activation(w_hi[:, c % 3, :], raw[:, c % 3, :], ACT.Copy).then_inc(hi_ready, 1)

            act.wait_ge(const_in, 64)
            act.wait_ge(c_zero, 1)
            act.activation(cpad[:, :, 0:NC], c_in[:, :, :], ACT.Silu).then_inc(c_ready, 1)
            act.wait_ge(const_ready, 2)
            act.activation(ones_r[:, :], ones[:, :], ACT.Copy).then_inc(const_ready, 1)
            act.wait_ge(x_in, 16)
            for n in range(KT // 2):
                if n >= 2:
                    act.wait_ge(x_sum, n - 1)
                act.activation((sq_t, bg_t)[n % 2][:, :, :], x_t[:, 2 * n:2 * n + 2, :], ACT.Square).then_inc(x_sq, 1)

            def ada_copy(p):
                for kind in range(2):
                    act.wait_ge(ada_used, 4 * p + 2 * kind + 2)
                    if not (isinstance(p, int) and p == 0):
                        act.wait_ge(sel_done, 2 * p - 1 + kind)
                    act.activation(part[:, kind, :], (TR, TV)[kind][:, 0:AW], ACT.Copy).then_inc(part_ready, 1)

            def split_h(p):
                act.wait_ge(hf_ready, 4 * p + 4)
                act.activation(h_hi[:, bass.ds(2 * p, 2), :], h_f[:, :, :], ACT.Copy).then_inc(h_hi_ready, 1)

            ada_copy(0)
            act.wait_ge(x_ms, 1)
            act.activation(rstd[:, :], O0[:, 0:NT], ACT.Sqrt, bias=eps_t[:, :], scale=1.0 / D_MODEL).then_inc(x_std, 1)
            split(0, 0)
            split_h(0)
            with act.Fori(1, 8) as p:
                ada_copy(p)
                split_h(p)
            split(0, 1)
            split(0, 2)

            def evac_qk(h, c):
                act.wait_ge(proj_done, 6 * h + c + 1)
                if not (isinstance(h, int) and 2 * h + c == 0):
                    act.wait_ge(rotated, 2 * h + c)
                bank = P[c % 2]
                act.activation(q_raw, bank[:, 0:NT], ACT.Copy).then_inc(qk_evac, 1)
                act.activation(work[0:64, 1, 0:NT], bank[64:128, 0:NT], ACT.Copy).then_inc(qk_evac, 1)
                act.activation(work[64:128, 1, 0:NT], bank[0:64, 0:NT], ACT.Copy).then_inc(qk_evac, 1)
                act.wait_ge(qk_evac, 3 * (2 * h + c) + 3)
                act.sem_inc(taken, 1)

            def evac_v(h, t):
                act.wait_ge(proj_done, 6 * h + t + 3)
                if not (isinstance(h, int) and h == 0):
                    act.wait_ge(step_a, h)
                act.activation(v_t[:, t, :], P[t][:, 0:NT], ACT.Copy).then_inc(v_ready, 1)
                act.wait_ge(v_ready, 2 * h + t + 1)
                act.sem_inc(taken, 1)

            def samples_v_hi(h):
                if not (isinstance(h, int) and h == 0):
                    act.wait_ge(diag_ready, 4 * h)
                act.activation(vs_hi[:, :, :], v_t[:, :, TP:NT], ACT.Copy).then_inc(vs_hi_ready, 1)

            def evac_bg(h, t):
                act.wait_ge(proj_done, 6 * h + t + 5)
                if not (isinstance(h, int) and h == 0):
                    act.wait_ge(yf_ready, 2 * h)
                act.activation(bg_t[:, t, :], P[t][:, 0:NT], ACT.Silu).then_inc(bg_ready, 1)
                act.wait_ge(bg_ready, 2 * h + t + 1)
                act.sem_inc(taken, 1)

            def evac_os(g):
                act.wait_ge(step_c1, g + 1)
                act.activation(scm[:, :], SC[:, :], ACT.Copy).then_inc(os_ready, 1)

            def square_root(g):
                act.wait_ge(step_f, g + 1)
                act.activation(rstd[:, :], O0[:, 0:NT], ACT.Sqrt, bias=eps_t[:, :], scale=1.0 / DV).then_inc(std_ready, 1)

            def y_hi(g):
                act.wait_ge(yf_ready, 2 * g + 2)
                act.activation(yb_hi[:, bass.ds(2 * g, 2), :], o_t[:, :, :], ACT.Copy).then_inc(yhi_ready, 1)

            def evac_b(h):
                act.wait_ge(step_b, h + 1)
                if not (isinstance(h, int) and h == 0):
                    act.wait_ge(ylo_ready, h)
                    act.wait_ge(sp_out, 16 * h)
                act.activation(o_t[:, 0, 0:TP], O0[:, 0:TP], ACT.Copy).then_inc(o_ready, 1)
                act.activation(o_t[:, 1, 0:TP], O1[:, 0:TP], ACT.Copy).then_inc(o_ready, 1)
                act.activation(sp_t[:, :], ST[:, 0:DV], ACT.Copy).then_inc(sp_ready, 1)

            def head(h, first=False):
                evac_qk(h, 0)
                split(h, 3)
                evac_qk(h, 1)
                if not first:
                    evac_os(h - 1)
                split(h, 4)
                evac_v(h, 0)
                split(h, 5)
                evac_v(h, 1)
                samples_v_hi(h)
                split(h, 6)
                if not first:
                    square_root(h - 1)
                split(h, 7)
                act.wait_ge(step_a, h + 1)
                if not first:
                    act.wait_ge(step_b, h)
                act.activation(v_nat[:, :], TV[:, :], ACT.Copy).then_inc(vnat_ready, 1)
                if not first:
                    y_hi(h - 1)
                evac_bg(h, 0)
                act.wait_ge(state_in, 16 * h + 16)
                act.wait_ge(head_in, 16 * h + 16)
                act.activation(s_t[:, :, :], s_t[:, :, :], ACT.Copy, scale=hc[:, HC_GAMMA:HC_GAMMA + 1]).then_inc(s_scaled, 1)
                evac_bg(h, 1)
                evac_b(h)
                split(h, 8)

            head(0, first=True)
            with act.Fori(1, H) as h:
                head(h)

            for g in range(4):
                for t in range(2):
                    act.wait_ge(proj_done, 49 + 4 * g + t)
                    if g >= 1:
                        act.wait_ge(npool_ready, g)
                        act.wait_ge(pooled_ready, 3 * g)
                    else:
                        act.wait_ge(const_ready, 3)
                    act.activation(ext[:, t, 16:16 + TP], P[t][:, 0:TP], ACT.Copy).then_inc(ax_evac, 1)
                    act.activation(exts[:, t, :, 15], P[t][:, TP:NT], ACT.Copy).then_inc(ax_evac, 1)
                    act.wait_ge(ax_evac, 4 * g + 2 * t + 2)
                    act.sem_inc(taken, 1)
                    if g == 0 and t == 1:
                        evac_os(H - 1)
                    if g == 1 and t == 0:
                        square_root(H - 1)
                    split(8, 4 * g + t + 3)
                if g == 1:
                    y_hi(H - 1)
                if g >= 1:
                    act.wait_ge(yaf_ready, 2 * g)
                    act.activation(ya_hi[:, 2 * g - 2:2 * g, :], ya_f[:, :, :], ACT.Copy).then_inc(yahi_ready, 1)
                for t in range(2):
                    act.wait_ge(proj_done, 51 + 4 * g + t)
                    if g == 0:
                        act.wait_ge(s_new, 4 * H)
                        act.wait_ge(qpad_ready, H)
                    else:
                        act.wait_ge(yaf_ready, 2 * g)
                    act.activation(sil_a[:, t, :], P[t][:, 0:NT], ACT.Silu).then_inc(sag_ready, 1)
                    act.wait_ge(sag_ready, 2 * g + t + 1)
                    act.sem_inc(taken, 1)
                    split(8, 4 * g + t + 5)
            act.wait_ge(yaf_ready, 8)
            act.activation(ya_hi[:, 6:8, :], ya_f[:, :, :], ACT.Copy).then_inc(yahi_ready, 1)

            act.wait_ge(ylo_ready, H)
            act.wait_ge(yalo_ready, 4)
            act.wait_ge(state_out, 16 * H)
            act.wait_ge(sp_out, 16 * H)
            act.wait_ge(spool_out, 64)
            act.wait_ge(ppool_out, 16)
            for u in range(8):
                for t in range(2):
                    n = 2 * u + t
                    act.wait_ge(proj_done, 65 + n)
                    act.activation(ya_out[:, n, :], P[t][:, 0:NT], ACT.Copy).then_inc(branch_ready, 1)
                    act.wait_ge(branch_ready, n + 1)
                    act.sem_inc(taken, 1)
                split(8, 19 + u)

            def merge_hi(n):
                act.wait_ge(mf_ready, n + 1)
                act.activation(m_hi[:, bass.ds(n, 1), :], m_f[:, :].unsqueeze(1), ACT.Copy).then_inc(mhi_ready, 1)

            def merge(it, first=False):
                a = 12 + it
                for c in range(6):
                    j, n = c % 3, 2 * it + c // 3
                    act.wait_ge(proj_done, 81 + 6 * it + c)
                    if not (first and c < 3):
                        act.wait_ge(mf_ready, n)
                    bank = P[c % 2][:, 0:NT]
                    if j == 0:
                        act.activation(sig_a[:, :], bank, ACT.Sigmoid, bias=vecs[:, bass.ds(V_BMERGE + n, 1)]).then_inc(branch_ready, 1)
                    elif j == 1:
                        act.activation(sig_b[:, :], bank, ACT.Sigmoid, bias=vecs[:, bass.ds(V_BMERGE + 16 + n, 1)]).then_inc(branch_ready, 1)
                    else:
                        act.activation(yb_out[:, :], bank, ACT.Copy).then_inc(branch_ready, 1)
                    act.wait_ge(branch_ready, 17 + 6 * it + c)
                    act.sem_inc(taken, 1)
                    if j == 0 and not (first and c == 0):
                        merge_hi(n - 1)
                    split(a, c + 3, after_ya=True)
                    if c == 4:
                        act.wait_ge(gate_used, 2 * it + 2)
                        act.activation(part[:, 0, :], TR[:, 0:AW], ACT.Copy).then_inc(gpart_ready, 1)

            merge(0, first=True)
            with act.Fori(1, 8) as it:
                merge(it)

            merge_hi(KT - 1)

            def out_tile(a, n, c):
                act.wait_ge(proj_done, 129 + n)
                act.activation(ya_out[:, bass.ds(n, 1), :], P[c % 2][:, 0:NT].unsqueeze(1), ACT.Copy).then_inc(out_evac, 1)
                act.wait_ge(out_evac, n + 1)
                act.sem_inc(taken, 1)
                if isinstance(a, int) and 6 * a + c + 3 >= 136:
                    return
                split(a, c + 3, after_ya=True)

            with act.Fori(0, 2) as m:
                for c in range(6):
                    out_tile(20 + m, 6 * m + c, c)
            for c in range(4):
                out_tile(22, 12 + c, c)
            act.wait_ge(out_ms, 1)
            act.activation(sig_a[:, :], O0[:, 0:NT], ACT.Sqrt, bias=eps_t[:, :], scale=1.0 / D_MODEL).then_inc(out_std, 1)

        @block.gpsimd
        def _(pool):
            def spread(h, half):
                for diag, vs in ((diag_hi, vs_hi), (diag_lo, vs_lo)):
                    v = vs[:, :, 4 * half:4 * half + 4].bitcast(f32).rearrange("p t b -> p b t").unsqueeze(3)
                    pool.tensor_tensor(diag[:, :, :, :], ident[:, :].unsqueeze(1).unsqueeze(1).to_broadcast([128, 4, 2, 128]),
                                       v.to_broadcast([128, 4, 2, 128]), ALU.mult).then_inc(diag_ready, 1)

            def head(h, first=False):
                if not first:
                    pool.wait_ge(step_b, h)
                    spread(h - 1, 1)
                    pool.wait_ge(cen_ready, 2 * h)
                    pool.tensor_tensor(sq_t[:, :, :], o_t[:, :, :], o_t[:, :, :], ALU.mult).then_inc(sq_ready, 1)
                    pool.wait_ge(sq_ready, h)
                    pool.tensor_tensor(osum[:, :], sq_t[:, 0, :], sq_t[:, 1, :], ALU.add).then_inc(sqs_ready, 1)
                    pool.wait_ge(step_c0, h)
                pool.wait_ge(vs_lo_ready, h + 1)
                spread(h, 0)

            pool.wait_ge(const_in, 64)
            head(0, first=True)
            with pool.Fori(1, H) as h:
                head(h)
            pool.wait_ge(step_b, H)
            spread(H - 1, 1)

            def windows(g):
                pool.wait_ge(ax_evac, 4 * g + 4)
                if g >= 1:
                    pool.wait_ge(pooled_ready, 3 * g)
                src, steps = ext, (1, 2, 4, 8)[:g + 1]
                for n, s in enumerate(steps):
                    dst = work[:, 2 * (n % 2):2 * (n % 2) + 2, :]
                    lo = 2 * s - 1
                    if n:
                        pool.wait_ge(win_step, sum(range(1, g + 1)) + n)
                    ins = pool.tensor_tensor(dst[:, :, lo:16 + TP], src[:, :, lo:16 + TP], src[:, :, lo - s:16 + TP - s], ALU.add)
                    ins.then_inc(win_step, 1)
                    src = dst

            windows(0)
            pool.wait_ge(cen_ready, 2 * H)
            pool.tensor_tensor(sq_t[:, :, :], o_t[:, :, :], o_t[:, :, :], ALU.mult).then_inc(sq_ready, 1)
            pool.wait_ge(sq_ready, H)
            pool.tensor_tensor(osum[:, :], sq_t[:, 0, :], sq_t[:, 1, :], ALU.add).then_inc(sqs_ready, 1)
            for g in range(1, 4):
                windows(g)

            pool.wait_ge(out_rstd, 1)
            pool.wait_ge(out_gated, 2 * KT)
            pool.wait_ge(x_again, 16)
            last = ya_out[:, 12:16, :]
            pool.tensor_tensor(last, last, yb_out[:, :].unsqueeze(1).to_broadcast([128, 4, NT]), ALU.mult).then_inc(y_scaled_p, 1)
            pool.wait_ge(y_scaled_p, 1)
            pool.tensor_tensor(last, last, x_late[:, 12:16, :], ALU.add).then_inc(y_ready_p, 1)

        @block.vector
        def _(dve):
            def split(a, c, after_ya=False):
                i = 6 * a + c
                dve.wait_ge(hi_ready, i + 1)
                if not isinstance(a, int):
                    dve.wait_ge(proj_done, outs(a, c - 2, after_ya))
                elif i >= 2:
                    dve.wait_ge(proj_done, outs(0, i - 2))
                dve.tensor_tensor(w_lo[:, c % 2, :], raw[:, c % 3, :], w_hi[:, c % 3, :].bitcast(f32), ALU.subtract).then_inc(lo_ready, 1)

            dve.memset(cpad[:, :, :], 0.0).then_inc(c_zero, 1)
            dve.memset(eps_t[:, :], EPS)
            dve.memset(ones[:, :], 1.0).then_inc(const_ready, 1)
            dve.memset(ext[:, :, 0:16], 0.0)
            dve.memset(qpad[:, :, :], 0.0).then_inc(const_ready, 1)
            for n in range(KT // 2):
                dve.wait_ge(x_sq, n + 1)
                pair = (sq_t, bg_t)[n % 2]
                if n == 0:
                    dve.tensor_tensor(osum[:, :], pair[:, 0, :], pair[:, 1, :], ALU.add).then_inc(x_sum, 1)
                else:
                    dve.tensor_tensor(pair[:, 0, :], pair[:, 0, :], pair[:, 1, :], ALU.add).then_inc(hs_mul, 1)
                    dve.wait_ge(hs_mul, n)
                    dve.wait_ge(x_sum, n)
                    dve.tensor_tensor(osum[:, :], osum[:, :], pair[:, 0, :], ALU.add).then_inc(x_sum, 1)
            dve.wait_ge(x_std, 1)
            dve.reciprocal(rstd[:, :], rstd[:, :]).then_inc(x_rstd, 1)
            dve.wait_ge(x_rstd, 1)
            for k in range(KT):
                ins = dve.scalar_tensor_tensor(out=x_t[:, k, :], in0=x_t[:, k, :], scalar=vecs[:, V_GPRE + k:V_GPRE + k + 1],
                                               in1=rstd[:, :], op0=ALU.mult, op1=ALU.mult)
                ins.then_inc(xn_ready, 1)

            HM = KT // 2 - 1

            def make_h(p):
                first = isinstance(p, int) and p == 0
                dve.wait_ge(sel_done, 2 * p + 2)
                if not first:
                    dve.wait_ge(hf_ready, 4 * p)
                for kind, mod in enumerate((mod_scale, mod_shift)):
                    at = V_ADAB + (16 if kind == 0 else 0)
                    bias = vecs[:, bass.ds(2 * p + at, 2)].unsqueeze(2).to_broadcast([128, 2, NC])
                    got = SC[:, 32 * kind:32 * kind + 32].rearrange("p (t n) -> p t n", t=2)[:, :, 0:NC]
                    dve.scalar_tensor_tensor(out=mod[:, :, :], in0=got, scalar=1.0 - kind, in1=bias,
                                             op0=ALU.add, op1=ALU.add).then_inc(mod_ready, 1)
                dve.wait_ge(mod_ready, 2 * p + 2)
                dve.wait_ge(xn_ready, KT)
                if not first:
                    dve.wait_ge(h_lo_ready, p)
                    dve.wait_ge(h_hi_ready, p)
                for t in range(2):
                    dve.tensor_scalar(h_f[:, t, 0:TP].unsqueeze(1), x_t[:, bass.ds(2 * p + t, 1), 0:TP], mod_scale[:, t, 0:1], mod_shift[:, t, 0:1],
                                      ALU.mult, ALU.add).then_inc(hf_ready, 1)
                dve.tensor_tensor(h_f[:, :, TP:NT], x_t[:, bass.ds(2 * p, 2), TP:NT], mod_scale[:, :, 1:NC], ALU.mult).then_inc(hf_ready, 1)
                dve.wait_ge(hf_ready, 4 * p + 3)
                dve.tensor_tensor(h_f[:, :, TP:NT], h_f[:, :, TP:NT], mod_shift[:, :, 1:NC], ALU.add).then_inc(hf_ready, 1)
                dve.wait_ge(h_hi_ready, p + 1)
                dve.tensor_tensor(h_lo[:, bass.ds(2 * p, 2), :], h_f[:, :, :], h_hi[:, bass.ds(2 * p, 2), :].bitcast(f32),
                                  ALU.subtract).then_inc(h_lo_ready, 1)

            make_h(0)
            split(0, 0)
            with dve.Fori(1, 8) as p:
                make_h(p)
            split(0, 1)
            dve.wait_ge(trig_in, 32)

            def rotate(h, c):
                n = 2 * h + c
                dve.wait_ge(qk_evac, 3 * n + 3)
                scale = 1.0 if c == 0 else DK ** -0.5
                if not (isinstance(h, int) and h == 0):
                    dve.wait_ge(step_a, h)
                dve.scalar_tensor_tensor(out=q_cos, in0=q_raw, scalar=scale, in1=trig_t[:, 0, :],
                                         op0=ALU.mult, op1=ALU.mult).then_inc(rot_mul, 1)
                dve.scalar_tensor_tensor(out=q_swap, in0=q_swap, scalar=scale, in1=trig_t[:, 1, :],
                                         op0=ALU.mult, op1=ALU.mult).then_inc(rot_mul, 1)
                dve.wait_ge(rot_mul, 2 * n + 2)
                dve.tensor_tensor(qk_t[:, c, :], q_cos, q_swap, ALU.add).then_inc(rotated, 1)

            def pad_q(h):
                dve.wait_ge(rotated, 2 * h + 1)
                if not (isinstance(h, int) and h == 0):
                    dve.wait_ge(step_c1, h)
                dve.tensor_copy(qpad[:, :, 0], qk_t[:, 0, TP:NT]).then_inc(qpad_ready, 1)

            def update_state(h, half):
                dve.wait_ge((step_b, step_c0)[half], h + 1)
                if half == 0:
                    dve.wait_ge(s_scaled, h + 1)
                for n, bank in enumerate((TR, TV)):
                    for m in range(2):
                        b = 4 * half + 2 * n + m
                        ins = dve.scalar_tensor_tensor(out=s_t[:, b, :], in0=bank[:, 256 * m:256 * m + 256], scalar=qk_t[:, 1, TP + b:TP + b + 1],
                                                       in1=s_t[:, b, :], op0=ALU.mult, op1=ALU.add)
                    ins.then_inc(s_new, 1)

            def collect(g):
                dve.wait_ge(step_d, g + 1)
                dve.wait_ge(o_ready, 2 * g + 2)
                src = ST[:, :].rearrange("p (i t j n) -> p t i j n", i=2, t=2, j=4)[:, :, :, :, 0]
                dst = o_t[:, :, TP:NT].rearrange("p t (i j) -> p t i j", i=2)
                dve.tensor_copy(dst, src).then_inc(o_samples, 1)
                dve.wait_ge(o_samples, g + 1)
                if not (isinstance(g, int) and g == 0):
                    dve.wait_ge(step_f, g)
                dve.tensor_tensor(osum[:, :], o_t[:, 0, :], o_t[:, 1, :], ALU.add).then_inc(osum_ready, 1)

            def centre(g):
                dve.wait_ge(step_e, g + 1)
                for t in range(2):
                    dve.scalar_tensor_tensor(out=o_t[:, t, :], in0=SC[:, 0:NT], scalar=-1.0 / DV, in1=o_t[:, t, :],
                                             op0=ALU.mult, op1=ALU.add).then_inc(cen_ready, 1)

            def norm(g):
                dve.wait_ge(std_ready, g + 1)
                dve.wait_ge(sqs_ready, g + 1)
                dve.reciprocal(rstd[:, :], rstd[:, :]).then_inc(rstd_ready, 1)
                dve.wait_ge(rstd_ready, g + 1)
                dve.wait_ge(bg_ready, 2 * g + 2)
                for t in range(2):
                    dve.scalar_tensor_tensor(out=o_t[:, t, :], in0=o_t[:, t, :], scalar=gn_cur[:, t:t + 1], in1=rstd[:, :],
                                             op0=ALU.mult, op1=ALU.mult).then_inc(ynorm_ready, 1)
                dve.wait_ge(ynorm_ready, 2 * g + 2)
                for t in range(2):
                    dve.tensor_tensor(o_t[:, t, :], o_t[:, t, :], bg_t[:, t, :], ALU.mult).then_inc(yf_ready, 1)

            def y_lo(g):
                dve.wait_ge(yhi_ready, g + 1)
                dve.tensor_tensor(yb_lo[:, bass.ds(2 * g, 2), :], o_t[:, :, :], yb_hi[:, bass.ds(2 * g, 2), :].bitcast(f32),
                                  ALU.subtract).then_inc(ylo_ready, 1)

            def decay(h):
                dve.wait_ge(step_a, h + 1)
                dve.wait_ge(head_in, 16 * h + 16)
                if not (isinstance(h, int) and h == 0):
                    dve.wait_ge(step_b, h)
                    dve.wait_ge(step_d, h)
                dve.tensor_tensor(scm[:, 0:256], SC[:, 0:256], hc[:, 0:256], ALU.mult).then_inc(scm_ready, 1)
                dve.tensor_tensor(scm[:, 256:384], SC[:, 256:384], hc[:, 0:128], ALU.mult).then_inc(scm_ready, 1)
                for c in range(2):
                    dve.tensor_scalar(kd[:, c, :], TR[:, 128 * c:128 * c + 128], hc[:, HC_KD0 + c:HC_KD0 + c + 1], None,
                                      ALU.mult).then_inc(kd_ready, 1)

            def head(h, first=False):
                rotate(h, 0)
                if not first:
                    update_state(h - 1, 1)
                split(h, 2)
                rotate(h, 1)
                pad_q(h)
                split(h, 3)
                if not first:
                    collect(h - 1)
                split(h, 4)
                dve.wait_ge(vs_hi_ready, h + 1)
                if not first:
                    dve.wait_ge(diag_ready, 4 * h)
                dve.tensor_tensor(vs_lo[:, :, :], v_t[:, :, TP:NT], vs_hi[:, :, :].bitcast(f32), ALU.subtract).then_inc(vs_lo_ready, 1)
                if not first:
                    centre(h - 1)
                split(h, 5)
                if not first:
                    norm(h - 1)
                decay(h)
                if not first:
                    y_lo(h - 1)
                split(h, 6)
                dve.tensor_copy(gn_cur[:, :], hc[:, HC_GN:HC_GN + 2]).then_inc(gn_saved, 1)
                update_state(h, 0)
                split(h, 7)

            head(0, first=True)
            with dve.Fori(1, H) as h:
                head(h)

            update_state(H - 1, 1)
            for g in range(4):
                w = WINDOWS[g]
                split(8, 4 * g + 2)
                dve.wait_ge(spool_in, 16 * g + 16)
                if g >= 1:
                    dve.wait_ge(npool_ready, g)
                dve.tensor_copy(exts[:, :, :, 0:15], sp_in[:, :, :, :]).then_inc(exts_old, 1)
                split(8, 4 * g + 3)
                if g == 0:
                    collect(H - 1)
                dve.wait_ge(ax_evac, 4 * g + 4)
                dve.wait_ge(exts_old, g + 1)
                if g == 0:
                    dve.wait_ge(step_a, H)
                else:
                    dve.wait_ge(pool_mm, g)
                    dve.wait_ge(spool_out, 16 * g)
                dve.tensor_reduce(win_s[:, :, :], exts[:, :, :, 16 - w:16], AX.X, ALU.add).then_inc(wins_ready, 1)
                dve.tensor_copy(npp_t[:, 2 * g:2 * g + 2, :], ext[:, :, 16 + TP - 15:16 + TP]).then_inc(ppool_ready, 1)
                dve.wait_ge(win_step, sum(range(1, g + 2)))
                win = work[:, 2 * (g % 2):2 * (g % 2) + 2, :]
                dve.scalar_tensor_tensor(out=pooled[:, :, 16:TP], in0=win[:, :, 32:16 + TP], scalar=1.0 / w,
                                         in1=ext[:, :, 32:16 + TP], op0=ALU.mult, op1=ALU.subtract).then_inc(pooled_ready, 1)
                count = cnt_t[:, g:g + 1, :].to_broadcast([128, 2, 16])
                dve.tensor_tensor(win[:, :, 16:32], win[:, :, 16:32], count, ALU.mult).then_inc(head_cols, 1)
                dve.wait_ge(head_cols, g + 1)
                dve.tensor_tensor(pooled[:, :, 0:16], win[:, :, 16:32], ext[:, :, 16:32], ALU.subtract).then_inc(pooled_ready, 1)
                dve.wait_ge(wins_ready, g + 1)
                dve.scalar_tensor_tensor(out=pooled[:, :, TP:NT], in0=win_s[:, :, :], scalar=1.0 / w, in1=exts[:, :, :, 15],
                                         op0=ALU.mult, op1=ALU.subtract).then_inc(pooled_ready, 1)
                dve.tensor_copy(nps_t[:, :, :, :], exts[:, :, :, 1:16]).then_inc(npool_ready, 1)
                split(8, 4 * g + 4)
                if g == 0:
                    centre(H - 1)
                split(8, 4 * g + 5)
                if g == 0:
                    norm(H - 1)
                    y_lo(H - 1)
                dve.wait_ge(pool_mm, g + 1)
                dve.wait_ge(sag_ready, 2 * g + 2)
                if g >= 1:
                    dve.wait_ge(yalo_ready, g)
                for t, bank in enumerate((O1, TR)):
                    dve.scalar_tensor_tensor(out=ya_f[:, t, :], in0=bank[:, 0:NT], scalar=vecs[:, V_PSCALE + 2 * g + t:V_PSCALE + 2 * g + t + 1],
                                             in1=sil_a[:, t, :], op0=ALU.mult, op1=ALU.mult).then_inc(yaf_ready, 1)
                dve.wait_ge(yahi_ready, g + 1)
                dve.tensor_tensor(ya_lo[:, 2 * g:2 * g + 2, :], ya_f[:, :, :], ya_hi[:, 2 * g:2 * g + 2, :].bitcast(f32),
                                  ALU.subtract).then_inc(yalo_ready, 1)

            for u in range(8):
                split(8, 18 + u)

            def merge_lo(n):
                dve.wait_ge(mhi_ready, n + 1)
                dve.tensor_tensor(m_lo[:, bass.ds(n, 1), :], m_f[:, :].unsqueeze(1), m_hi[:, bass.ds(n, 1), :].bitcast(f32),
                                  ALU.subtract).then_inc(mlo_ready, 1)

            def merge(it, first=False):
                a = 12 + it
                for c in range(6):
                    if c % 3 == 2:
                        n = 2 * it + c // 3
                        dve.wait_ge(branch_ready, 17 + 6 * it + c)
                        if not (first and c == 2):
                            dve.wait_ge(mlo_ready, n)
                        dve.tensor_tensor(sig_a[:, :].unsqueeze(1), sig_a[:, :].unsqueeze(1), ya_out[:, bass.ds(n, 1), :], ALU.mult).then_inc(merge_mul, 1)
                        dve.tensor_tensor(sig_b[:, :], sig_b[:, :], yb_out[:, :], ALU.mult).then_inc(merge_mul, 1)
                        dve.wait_ge(merge_mul, 2 * n + 2)
                        dve.tensor_tensor(m_f[:, :], sig_a[:, :], sig_b[:, :], ALU.add).then_inc(mf_ready, 1)
                    split(a, c + 2, after_ya=True)
                    if c % 3 == 0 and not (first and c == 0):
                        merge_lo(2 * it + c // 3 - 1)
                dve.wait_ge(gsel_done, it + 1)
                tiles = bass.ds(2 * it, 2)
                got = SC[:, 0:32].rearrange("p (t n) -> p t n", t=2)[:, :, 0:NC]
                bias = vecs[:, bass.ds(2 * it + V_ADAB + 32, 2)].unsqueeze(2).to_broadcast([128, 2, NC])
                post = vecs[:, bass.ds(2 * it + V_GPOST, 2)].unsqueeze(2).to_broadcast([128, 2, NC])
                dve.tensor_tensor(mod_scale[:, :, :], got, bias, ALU.add).then_inc(gbias_ready, 1)
                dve.wait_ge(gbias_ready, it + 1)
                dve.tensor_tensor(gate_g[:, tiles, :], mod_scale[:, :, :], post, ALU.mult).then_inc(gate_ready, 1)

            merge(0, first=True)
            with dve.Fori(1, 8) as it:
                merge(it)
            merge_lo(KT - 1)

            def out_tile(a, n, c, first=False):
                dve.wait_ge(out_evac, n + 1)
                tile = bass.ds(n, 1)
                o = ya_out[:, tile, :]
                if not first:
                    dve.wait_ge(out_acc, n)
                dve.tensor_tensor(sig_a[:, :].unsqueeze(1), o, o, ALU.mult).then_inc(out_sq, 1)
                dve.wait_ge(out_sq, n + 1)
                if first:
                    dve.tensor_copy(sig_b[:, :], sig_a[:, :]).then_inc(out_acc, 1)
                else:
                    dve.tensor_tensor(sig_b[:, :], sig_b[:, :], sig_a[:, :], ALU.add).then_inc(out_acc, 1)
                dve.tensor_tensor(ya_out[:, tile, 0:TP], ya_out[:, tile, 0:TP], gate_g[:, tile, 0:1].to_broadcast([128, 1, TP]),
                                  ALU.mult).then_inc(out_gated, 1)
                dve.tensor_tensor(ya_out[:, tile, TP:NT], ya_out[:, tile, TP:NT], gate_g[:, tile, 1:NC], ALU.mult).then_inc(out_gated, 1)
                if isinstance(a, int) and 6 * a + c + 2 >= 136:
                    return
                split(a, c + 2, after_ya=True)

            dve.wait_ge(gate_ready, 8)
            out_tile(20, 0, 0, first=True)
            for c in range(1, 6):
                out_tile(20, c, c)
            for c in range(6):
                out_tile(21, 6 + c, c)
            for c in range(4):
                out_tile(22, 12 + c, c)
            dve.wait_ge(out_std, 1)
            dve.reciprocal(yb_out[:, :], sig_a[:, :]).then_inc(out_rstd, 1)
            dve.wait_ge(out_rstd, 1)
            dve.wait_ge(out_gated, 2 * KT)
            dve.wait_ge(x_again, 16)
            for q in range(3):
                y = ya_out[:, 4 * q:4 * q + 4, :]
                dve.tensor_tensor(y, y, yb_out[:, :].unsqueeze(1).to_broadcast([128, 4, NT]), ALU.mult).then_inc(y_scaled, 1)
                dve.wait_ge(y_scaled, q + 1)
                dve.tensor_tensor(y, y, x_late[:, 4 * q:4 * q + 4, :], ALU.add).then_inc(y_ready, 1)


def constants():
    f = np.float32
    m = np.arange(128)
    head = np.zeros((H, 128, TP + 3))
    for h in range(H):
        lg = np.log1p(-(2.0 ** (-5.0 - h)))
        d = np.arange(TP)[None, :] - m[:, None]
        head[h, :, 0:TP] = np.where(d >= 0, np.exp(np.maximum(d, 0) * lg), 0.0)
        head[h, :, HC_KD0] = np.exp((TP - 1 - m) * lg)
        head[h, :, HC_KD1] = np.exp((127 - m) * lg)
        head[h, :, HC_GAMMA] = np.exp(lg)
    half = DK // 2
    inv = (10000.0 ** (-np.arange(half, dtype=f) / f(half))).astype(f)
    pos = np.concatenate([np.arange(TP), np.full(TS, PAST_LEN)]).astype(f)
    ang = (pos[None, :] * inv[:, None]).astype(f).astype(np.float64)
    cos, sin = np.cos(ang), np.sin(ang)
    trig = np.stack([np.concatenate([cos, cos]), np.concatenate([-sin, sin])], axis=1)
    sel = np.zeros((128, NC))
    for j in range(4):
        sel[32 * j + np.arange(NC), np.arange(NC)] = 1.0
    cnt = np.stack([1.0 / np.minimum(np.arange(16) + 1, w) for w in WINDOWS])
    cnt = np.broadcast_to(cnt, (128, 4, 16))
    return head.astype(f), trig.astype(f), np.eye(128, dtype=f), sel.astype(f), np.ascontiguousarray(cnt, dtype=f)


def kernel(x_prompt, x_sample, state_pool, state_ret, c_prompt, c_sample, ada_w, ada_b, g_pre, g_post,
           w_in, pool_w, pool_scale, gn_g, w_a_proj, w_b_proj, w_merge, b_merge, w_out):
    import concourse.bacc as bacc
    from concourse.bass_utils import run_bass_kernel_spmd

    A = lambda x: np.asarray(x)
    tiles = lambda v: A(v).reshape(-1, 128).T
    feat = lambda m: m.reshape(m.shape[0], -1, 128).transpose(2, 1, 0)
    block = lambda w, c: w[:, c:c + 128].reshape(-1, 128, 128).transpose(1, 0, 2).reshape(128, -1)

    win, wm, wa, wb, wo = A(w_in)[0], A(w_merge)[0], A(w_a_proj)[0], A(w_b_proj)[0], A(w_out)[0]
    units = []
    Q0, K0, V0, B0 = 2 * D_POOL, 2 * D_POOL + H * DK, 2 * D_POOL + 2 * H * DK, 2 * D_POOL + 2 * H * DK + H * DV
    for h in range(H):
        for c in (Q0 + DK * h, K0 + DK * h, V0 + DV * h, V0 + DV * h + 128, B0 + DV * h, B0 + DV * h + 128):
            units.append(block(win, c))
    for g in range(4):
        for c in (256 * g, 256 * g + 128, D_POOL + 256 * g, D_POOL + 256 * g + 128):
            units.append(block(win, c))
    for u in range(8):
        units.append(np.concatenate([block(wa, 256 * u), block(wa, 256 * u + 128)], axis=1))
    for n in range(KT):
        units += [block(wm, 128 * n), block(wm, D_MODEL + 128 * n), block(wb, 128 * n)]
    for n in range(KT):
        units.append(block(wo, 128 * n))
    stream = np.stack(units)

    aw = A(ada_w)[0]

    def ada_units(c):
        w = aw[:, c:c + AW].reshape(2, 8, 128, AW).transpose(0, 2, 1, 3).reshape(2, 128, UNIT)
        return [w[0], w[1]]
    ada0 = np.stack([u for p in range(8) for c in (D_MODEL + AW * p, AW * p) for u in ada_units(c)])
    ada1 = np.stack([u for p in range(8) for u in ada_units(2 * D_MODEL + AW * p)])

    head, trig, ident, sel, cnt = constants()
    gn = A(gn_g)[0].reshape(H, 2, 128).transpose(0, 2, 1)
    ins = {
        "stream": stream, "ada0": ada0, "ada1": ada1,
        "xT": np.concatenate([feat(A(x_prompt)[0]), feat(A(x_sample)[:, 0])], axis=2),
        "cT": np.concatenate([feat(A(c_prompt)), feat(A(c_sample))], axis=2),
        "vec": np.concatenate([tiles(A(g_pre)[0]), tiles(A(g_post)[0]), tiles(A(ada_b)[0]), tiles(A(b_merge)[0]),
                               tiles(A(pool_scale)[0])], axis=1),
        "headc": np.concatenate([head, gn], axis=2), "trig": trig, "ident_in": ident, "sel_in": sel, "cnt_in": cnt,
        "poolw": A(pool_w)[0].reshape(4, 2, 128, 256).transpose(0, 2, 1, 3).reshape(4, 128, 512),
        "spool": A(state_pool)[0].reshape(TS, POOL_BUF, 4, 2, 128).transpose(2, 4, 3, 0, 1),
        "sret": A(state_ret)[0].transpose(1, 2, 0, 3),
    }
    outputs = {"yT": (128, KT, NT), "npool_p": (128, 8, POOL_BUF), "npool_s": (4, 128, 2, TS, POOL_BUF),
               "nret_p": (H, 128, DV), "nret_s": (H, 128, TS, DV)}
    nc = bacc.Bacc("TRN2", target_bir_lowering=False, num_devices=1)
    arrays, aps = {}, {}
    for name, a in ins.items():
        arrays[name] = np.ascontiguousarray(a)
        aps[name] = nc.dram_tensor(name, a.shape, mybir.dt.from_np(a.dtype), kind="ExternalInput").ap()
    for name, shape in outputs.items():
        aps[name] = nc.dram_tensor(name, shape, mybir.dt.float32, kind="ExternalOutput").ap()
    build(nc, **aps)
    r = run_bass_kernel_spmd(nc, [arrays], core_ids=[0]).results[0]
    y = r["yT"].transpose(2, 1, 0).reshape(NT, D_MODEL)
    return (y[:TP].reshape(1, TP, D_MODEL), y[TP:].reshape(TS, 1, D_MODEL),
            r["npool_p"].transpose(2, 1, 0).reshape(1, 1, POOL_BUF, D_POOL),
            r["nret_p"].reshape(1, 1, H, DK, DV),
            r["npool_s"].transpose(3, 4, 0, 2, 1).reshape(1, TS, POOL_BUF, D_POOL),
            r["nret_s"].transpose(2, 0, 1, 3).reshape(1, TS, H, DK, DV))
```

```python
import numpy as np
import concourse.bass as bass
from concourse import mybir
from contextlib import ExitStack

D_MODEL = 2048
TP = 256
TS = 8
NT = TP + TS
KT = D_MODEL // 128
NC = 1 + TS
D_POOL = D_MODEL // 2
WINDOWS = (2, 4, 8, 16)
POOL_BUF = max(WINDOWS) - 1
H = 8
DK = D_MODEL // 16
DV = D_MODEL // 8
PAST_LEN = 2048
EPS = 1e-6
UNIT = KT * 128
AW = 256
V_GPRE, V_GPOST, V_ADAB, V_BMERGE, V_PSCALE = 0, 16, 32, 80, 112
V_N = 120
HC_KD0, HC_KD1, HC_GAMMA, HC_GN = TP, TP + 1, TP + 2, TP + 3
HC_N = TP + 5
Y_DVE, Y_POOL = ((0, 4), (4, 8), (8, 10), (10, 11)), ((11, 14), (14, 16))


def outs(a, c, after_ya=False):
    i = 6 * a + c
    if not isinstance(a, int):
        return i + (9 if after_ya else 1)
    return i + 1 if i < 64 else (64 + 2 * (i - 63) if i < 72 else i + 9)


def build(nc, stream, ada0, ada1, xT, cT, vec, headc, trig, ident_in, ident2_in, sel_in, cnt_in, poolw, spool,
          sret, yT, npool_p, npool_s, nret_p, nret_s):
    f32, f32r = mybir.dt.float32, mybir.dt.float32r
    ALU, ACT, AX = mybir.AluOpType, mybir.ActivationFunctionType, mybir.AxisListType

    ctx = ExitStack()
    with ctx:
        def sb(name, shape, dt=f32, stack=ctx):
            return stack.enter_context(nc.sbuf_tensor(name, shape, dt))

        def sem(name):
            return ctx.enter_context(nc.semaphore(name))

        raw = sb("raw", [128, 3, UNIT])
        w_hi = sb("w_hi", [128, 3, UNIT], f32r)
        w_lo = sb("w_lo", [128, 2, UNIT], f32r)
        h_hi = sb("h_hi", [128, KT, NT], f32r)
        h_lo = sb("h_lo", [128, KT, NT], f32r)
        cpad = sb("cpad", [128, KT, 32])
        c_in = sb("c_in", [128, KT, NC])
        part = sb("part", [128, 2, AW])
        vecs = sb("vecs", [128, V_N])
        ident = sb("ident", [128, 128])
        ident2 = sb("ident2", [128, 64])
        ones = sb("ones", [128, 128])
        sel = sb("sel", [128, NC])
        eps_t = sb("eps_t", [128, 1])
        eps_sqrt = sb("eps_sqrt", [128, 1])
        mod_scale = sb("mod_scale", [128, 2, NC])
        mod_shift = sb("mod_shift", [128, 2, NC])
        gate_g = sb("gate_g", [128, KT, NC])
        early = ExitStack()
        ada_ring = sb("ada_ring", [128, 4, UNIT], f32, early)
        x_t = sb("x_t", [128, KT, NT], f32, early)
        early.close()
        yb_hi = sb("yb_hi", [128, KT, NT], f32r)
        yb_lo = sb("yb_lo", [128, KT, NT], f32r)
        mid = ExitStack()
        ya_hi = sb("ya_hi", [128, KT // 2, NT], f32r, mid)
        ya_lo = sb("ya_lo", [128, KT // 2, NT], f32r, mid)
        work = sb("work", [128, 4, 16 + TP], f32, mid)
        qk_t = sb("qk_t", [128, 2, NT], f32, mid)
        v_t = sb("v_t", [128, 2, NT], f32, mid)
        scm = sb("scm", [128, 512], f32, mid)
        v_nat = sb("v_nat", [128, 512], f32, mid)
        kd = sb("kd", [128, 2, 128], f32, mid)
        v_blocks = sb("v_blocks", [128, 4, TS], f32, mid)
        v_parts = sb("v_parts", [128, 4, TS], f32r, mid)
        diag = sb("diag", [128, TS, 4, 64], f32r, mid)
        ones_r = sb("ones_r", [128, 128], f32r, mid)
        s_t = sb("s_t", [128, TS, DV], f32, mid)
        sp_t = sb("sp_t", [128, DV], f32, mid)
        o_t = sb("o_t", [128, 2, NT], f32, mid)
        sq_t = sb("sq_t", [128, 2, NT], f32, mid)
        osum = sb("osum", [128, NT], f32, mid)
        rstd = sb("rstd", [128, NT], f32, mid)
        bg_t = sb("bg_t", [128, 2, NT], f32, mid)
        qpad = sb("qpad", [128, TS, 32], f32, mid)
        trig_t = sb("trig_t", [128, 2, NT], f32, mid)
        hc = sb("hc", [128, HC_N], f32, mid)
        gn_cur = sb("gn_cur", [128, 2], f32, mid)
        ext = sb("ext", [128, 2, 16 + TP], f32, mid)
        exts = sb("exts", [128, 2, TS, 16], f32, mid)
        sp_in = sb("sp_in", [128, 2, TS, POOL_BUF], f32, mid)
        nps_t = sb("nps_t", [128, 2, TS, POOL_BUF], f32, mid)
        npp_t = sb("npp_t", [128, 8, POOL_BUF], f32, mid)
        cnt_t = sb("cnt_t", [128, 4, 16], f32, mid)
        win_s = sb("win_s", [128, 2, TS], f32, mid)
        mid.close()
        late = ExitStack()
        m_hi = sb("m_hi", [128, KT, NT], f32r, late)
        ya_out = sb("ya_out", [128, KT, NT], f32, late)
        m_lo = sb("m_lo", [128, KT, NT], f32r, late)
        gate_ring = sb("gate_ring", [128, 2, UNIT], f32, late)
        sig_a = sb("sig_a", [128, NT], f32, late)
        sig_b = sb("sig_b", [128, NT], f32, late)
        yb_out = sb("yb_out", [128, NT], f32, late)
        m_f = sb("m_f", [128, NT], f32, late)
        late.close()
        h_f = v_t
        q_raw, q_swap, q_cos = work[:, 0, 0:NT], work[:, 1, 0:NT], work[:, 2, 0:NT]
        pooled, pool_w, sil_a, ya_f = v_t, v_nat, qk_t, trig_t

        banks = [ctx.enter_context(nc.psum_tensor(f"bank{n}", [128, 512], f32)) for n in range(8)]
        P = banks[0:2]
        TR, TV, SC, O0, O1, ST = banks[2:8]

        const_in = sem("const_in")
        x_in = sem("x_in")
        trig_in = sem("trig_in")
        raw_loaded = [sem(f"raw_loaded{s}") for s in range(3)]
        hi_ready, lo_ready = sem("hi_ready"), sem("lo_ready")
        proj_done, taken = sem("proj_done"), sem("taken")
        ada_loaded = [sem(f"ada_loaded{s}") for s in range(4)]
        ada_used, part_ready, sel_done = sem("ada_used"), sem("part_ready"), sem("sel_done")
        mod_ready, hf_ready, h_hi_ready, h_lo_ready = sem("mod_ready"), sem("hf_ready"), sem("h_hi_ready"), sem("h_lo_ready")
        c_zero, c_ready, const_ready = sem("c_zero"), sem("c_ready"), sem("const_ready")
        x_sq, x_sum, x_ms, x_std, x_rstd, xn_ready = (sem("x_sq"), sem("x_sum"), sem("x_ms"), sem("x_std"),
                                                      sem("x_rstd"), sem("xn_ready"))
        hs_mul = sem("hs_mul")
        head_in, state_in, state_out, sp_out = sem("head_in"), sem("state_in"), sem("state_out"), sem("sp_out")
        rot_mul, rotated, qpad_ready = sem("rot_mul"), sem("rotated"), sem("qpad_ready")
        vs_hi_ready, vs_lo_ready, diag_ready = sem("vs_hi_ready"), sem("vs_lo_ready"), sem("diag_ready")
        step_a, step_b, step_c0, step_c1, step_d, step_e, step_f = (sem(f"step_{x}") for x in ("a", "b", "c0", "c1", "d", "e", "f"))
        vnat_ready, kd_ready, scm_ready = sem("vnat_ready"), sem("kd_ready"), sem("scm_ready")
        o_ready, sp_ready, s_scaled, s_new, os_ready = sem("o_ready"), sem("sp_ready"), sem("s_scaled"), sem("s_new"), sem("os_ready")
        o_samples, osum_ready, cen_ready, sq_ready, sqs_ready = (sem("o_samples"), sem("osum_ready"), sem("cen_ready"),
                                                                 sem("sq_ready"), sem("sqs_ready"))
        std_ready, rstd_ready, ynorm_ready, yf_ready, yhi_ready, ylo_ready, gn_saved = (
            sem("std_ready"), sem("rstd_ready"), sem("ynorm_ready"), sem("yf_ready"), sem("yhi_ready"), sem("ylo_ready"), sem("gn_saved"))
        spool_in, poolw_in, spool_out = sem("spool_in"), sem("poolw_in"), sem("spool_out")
        exts_old, win_ready, win_step, wins_ready = sem("exts_old"), sem("win_ready"), sem("win_step"), sem("wins_ready")
        head_cols, pooled_ready, pool_mm = sem("head_cols"), sem("pooled_ready"), sem("pool_mm")
        yaf_ready, yahi_ready, yalo_ready, npool_ready, ppool_ready, ppool_out = (
            sem("yaf_ready"), sem("yahi_ready"), sem("yalo_ready"), sem("npool_ready"), sem("ppool_ready"), sem("ppool_out"))
        gate_loaded = [sem(f"gate_loaded{s}") for s in range(2)]
        gate_used, gpart_ready, gsel_done, gbias_ready, gate_ready = (
            sem("gate_used"), sem("gpart_ready"), sem("gsel_done"), sem("gbias_ready"), sem("gate_ready"))
        merge_mul, mf_ready, mhi_ready, mlo_ready = (
            sem("merge_mul"), sem("mf_ready"), sem("mhi_ready"), sem("mlo_ready"))
        out_sq, out_acc, out_gated, out_ms, out_std, out_rstd = (
            sem("out_sq"), sem("out_acc"), sem("out_gated"), sem("out_ms"), sem("out_std"), sem("out_rstd"))
        x_again, y_scaled, y_ready, y_out = sem("x_again"), sem("y_scaled"), sem("y_ready"), sem("y_out")
        y_scaled_p, y_ready_p = sem("y_scaled_p"), sem("y_ready_p")
        x_late = raw[:, :, :].rearrange("p s n -> p (s n)")[:, 0:KT * NT].rearrange("p (k t) -> p k t", k=KT)

        block = ctx.enter_context(nc.Block())

        @block.sync
        def _(sp):
            def load(a, c):
                i = 6 * a + c
                if not isinstance(a, int) or i >= 3:
                    sp.wait_ge(lo_ready, i - 2)
                sp.dma_start(raw[:, c % 3, :], stream[i]).then_inc(raw_loaded[c % 3], 16)

            sp.dma_start(c_in[:, :, :], cT).then_inc(const_in, 16)
            sp.dma_start(vecs[:, :], vec).then_inc(const_in, 16)
            sp.dma_start(ident[:, :], ident_in).then_inc(const_in, 16)
            sp.dma_start(sel[:, :], sel_in).then_inc(const_in, 16)
            sp.dma_start(ident2[:, :], ident2_in).then_inc(const_in, 16)
            sp.dma_start(x_t[:, :, :], xT).then_inc(x_in, 16)
            for s in range(4):
                sp.dma_start(ada_ring[:, s, :], ada0[s]).then_inc(ada_loaded[s], 16)
            load(0, 0)
            sp.dma_start(trig_t[:, :, :], trig).then_inc(trig_in, 16)
            sp.dma_start(cnt_t[:, :, :], cnt_in).then_inc(trig_in, 16)
            sp.dma_start(hc[:, :], headc[0]).then_inc(head_in, 16)

            def ada_load(p):
                for s in range(4):
                    sp.wait_ge(ada_used, 4 * p + s - 3)
                    sp.dma_start(ada_ring[:, s, :], ada0[4 * p + s]).then_inc(ada_loaded[s], 16)

            with sp.Fori(1, 7) as p:
                ada_load(p)
            load(0, 1)
            ada_load(7)
            load(0, 2)
            sp.dma_start(s_t[:, :, :], sret[0]).then_inc(state_in, 16)
            for c in range(3, 9):
                load(0, c)

            def head_stores(g):
                sp.wait_ge(sp_ready, g + 1)
                sp.dma_start(nret_p[g], sp_t[:, :]).then_inc(sp_out, 16)
                sp.wait_ge(s_new, 4 * g + 4)
                sp.dma_start(nret_s[g], s_t[:, :, :]).then_inc(state_out, 16)

            with sp.Fori(1, H) as h:
                for c in range(6):
                    if c == 2:
                        sp.wait_ge(gn_saved, h)
                        sp.wait_ge(s_scaled, h)
                        sp.dma_start(hc[:, :], headc[h]).then_inc(head_in, 16)
                    if c == 4:
                        head_stores(h - 1)
                    if c == 5:
                        sp.wait_ge(state_out, 16 * h)
                        sp.wait_ge(step_c1, h)
                        sp.dma_start(s_t[:, :, :], sret[h]).then_inc(state_in, 16)
                    load(h, c + 3)
            for i in range(51, 75):
                g, r = divmod(i - 51, 4)
                if g < 4 and r == 2:
                    if g >= 1:
                        sp.wait_ge(exts_old, g)
                    sp.dma_start(sp_in[:, :, :, :], spool[g]).then_inc(spool_in, 16)
                    if g == 0:
                        sp.wait_ge(step_b, H)
                    else:
                        sp.wait_ge(pool_mm, g)
                    sp.dma_start(pool_w[:, :], poolw[g]).then_inc(poolw_in, 16)
                if i == 52:
                    head_stores(H - 1)
                if r == 1 and 1 <= g <= 4:
                    sp.wait_ge(npool_ready, g)
                    sp.dma_start(npool_s[g - 1], nps_t[:, :, :, :]).then_inc(spool_out, 16)
                if i == 68:
                    sp.wait_ge(ppool_ready, 4)
                    sp.dma_start(npool_p, npp_t[:, :, :]).then_inc(ppool_out, 16)
                load(8, i - 48)
            sp.wait_ge(ylo_ready, H)
            sp.wait_ge(yalo_ready, 4)
            sp.wait_ge(state_out, 16 * H)
            sp.wait_ge(sp_out, 16 * H)
            sp.wait_ge(spool_out, 64)
            sp.wait_ge(ppool_out, 16)
            for s in range(2):
                sp.dma_start(gate_ring[:, s, :], ada1[s]).then_inc(gate_loaded[s], 16)
            with sp.Fori(0, 7) as it:
                for c in range(6):
                    load(12 + it, c + 3)
                    if c in (4, 5):
                        s = c - 4
                        sp.wait_ge(gate_used, 2 * it + s + 1)
                        sp.dma_start(gate_ring[:, s, :], ada1[2 * it + 2 + s]).then_inc(gate_loaded[s], 16)
            for c in range(6):
                load(19, c + 3)
            for i in range(123, 136):
                load(20, i - 120)
            sp.wait_ge(lo_ready, 136)
            sp.dma_start(x_late, xT).then_inc(x_again, 16)
            for q in range(len(Y_DVE)):
                if q < len(Y_POOL):
                    sp.wait_ge(y_ready_p, q + 1)
                    k0, k1 = Y_POOL[q]
                    sp.dma_start(yT[:, k0:k1, :], ya_out[:, k0:k1, :]).then_inc(y_out, 16)
                sp.wait_ge(y_ready, q + 1)
                k0, k1 = Y_DVE[q]
                sp.dma_start(yT[:, k0:k1, :], ya_out[:, k0:k1, :]).then_inc(y_out, 16)
            sp.wait_ge(y_out, 16 * (len(Y_DVE) + len(Y_POOL)))

        @block.tensor
        def _(pe):
            def ada_unit(bank, w, half):
                for k in range(8):
                    j = k % 4
                    mm = pe.matmul(bank[32 * j:32 * j + 32, 0:AW], cpad[:, 8 * half + k, :],
                                   w[:, AW * k:AW * k + AW], start=(half == 0 and k < 4),
                                   stop=(half == 1 and k >= 4), tile_position=(0, 32 * j))
                return mm

            def select(bank, kind):
                for t in range(2):
                    col = (2 * kind + t) * 16
                    mm = pe.matmul(bank[:, col:col + NC], part[:, kind, 128 * t:128 * t + 128], sel[:, :],
                                   start=True, stop=True)
                return mm

            def products(c, par, hi, lo, ks, depth=KT, m=0):
                out = P[par][:, 0:NT]
                for k in ks:
                    col = (m * depth + k) * 128
                    wh, wl = w_hi[:, c % 3, col:col + 128], w_lo[:, c % 2, col:col + 128]
                    pe.matmul(out, wh, hi[:, k, :], start=(k == 0), stop=False)
                    pe.matmul(out, wh, lo[:, k, :], start=False, stop=False)
                    mm = pe.matmul(out, wl, hi[:, k, :], start=False, stop=(k == depth - 1))
                return mm

            def project(a, c, hi, lo, depth=KT, parts=1, after_ya=False, last=None):
                i = 6 * a + c
                pe.wait_ge(lo_ready, i + 1)
                first = outs(a, c, after_ya) - parts
                for m in range(parts):
                    par = (c + m) % 2 if parts == 1 else m % 2
                    if not isinstance(a, int) or first + m >= 2:
                        pe.wait_ge(taken, first + m - 1)
                    if last and m == 0:
                        products(c, par, hi, lo, range(last[0]), depth, m)
                        pe.wait_ge(last[1], last[2])
                        products(c, par, hi, lo, range(last[0], depth), depth, m).then_inc(proj_done, 1)
                    else:
                        products(c, par, hi, lo, range(depth), depth, m).then_inc(proj_done, 1)

            pe.wait_ge(const_in, 80)
            pe.wait_ge(c_ready, 1)
            pe.wait_ge(const_ready, 1)

            def ada_pair(p):
                for s in range(4):
                    kind, half = divmod(s, 2)
                    pe.wait_ge(ada_loaded[s], 16 * p + 16)
                    if half == 0 and p > 0:
                        pe.wait_ge(part_ready, 2 * p - 1 + kind)
                    ada_unit((TR, TV)[kind], ada_ring[:, s, :], half).then_inc(ada_used, 1)
                if p > 0:
                    pe.wait_ge(mod_ready, 2 * p)
                for kind in range(2):
                    pe.wait_ge(part_ready, 2 * p + 1 + kind)
                    select(SC, kind).then_inc(sel_done, 1)

            pe.wait_ge(x_sum, KT // 2)
            pe.matmul(O0[:, 0:NT], ones[:, :], osum[:, :], start=True, stop=True).then_inc(x_ms, 1)
            ada_pair(0)
            pe.wait_ge(lo_ready, 1)
            for p in range(1, 8):
                ada_pair(p)
                ready = (0, 0, 0, 2, 4, 5, 6, 7)[p]
                if ready:
                    pe.wait_ge(h_lo_ready, ready)
                    used = (0, 0, 0, 0, 2, 4, 5, 6)[p]
                    products(0, 0, h_hi, h_lo, range(2 * used, 2 * ready))
            pe.wait_ge(lo_ready, 2)
            products(1, 1, h_hi, h_lo, range(KT - 2))
            pe.wait_ge(h_lo_ready, 8)
            products(0, 0, h_hi, h_lo, range(KT - 2, KT)).then_inc(proj_done, 1)
            products(1, 1, h_hi, h_lo, range(KT - 2, KT)).then_inc(proj_done, 1)

            def a_step(h):
                pe.wait_ge(rotated, 2 * h + 2)
                pe.wait_ge(taken, 6 * h + 4)
                if not (isinstance(h, int) and h == 0):
                    pe.wait_ge(s_new, 4 * h)
                    pe.wait_ge(cen_ready, 2 * h)
                q, k = qk_t[:, 0, :], qk_t[:, 1, :]
                for c in range(2):
                    pe.transpose(TR[:, 128 * c:128 * c + 128], k[:, 128 * c:128 * c + 128], ident[:, :])
                for c in range(2):
                    for t in range(2):
                        pe.transpose(TV[:, 256 * c + 128 * t:256 * c + 128 * t + 128],
                                     v_t[:, t, 128 * c:128 * c + 128], ident[:, :])
                pe.matmul(SC[:, 0:256], k[:, 0:128], q[:, 0:256], start=True, stop=True)
                pe.matmul(SC[:, 256:384], k[:, 128:256], q[:, 128:256], start=True, stop=True).then_inc(step_a, 1)

            def spread_v(n, bank):
                return pe.matmul(bank[:, :], ones_r[:, :], diag[:, 2 * n:2 * n + 2, :, :].rearrange("p b q n -> p (b q n)"),
                                 start=True, stop=True)

            def b_step(h):
                pe.wait_ge(vnat_ready, h + 1)
                pe.wait_ge(scm_ready, 2 * h + 2)
                if not (isinstance(h, int) and h == 0):
                    pe.wait_ge(std_ready, h)
                    pe.wait_ge(o_ready, 2 * h)
                for t, bank in enumerate((O0, O1)):
                    pe.matmul(bank[:, 0:256], v_nat[:, 128 * t:128 * t + 128], scm[:, 0:256], start=True, stop=False)
                    mm = pe.matmul(bank[:, 128:256], v_nat[:, 256 + 128 * t:384 + 128 * t], scm[:, 256:384],
                                   start=False, stop=True)
                pe.wait_ge(kd_ready, 2 * h + 2)
                if not (isinstance(h, int) and h == 0):
                    pe.wait_ge(o_samples, h)
                pe.matmul(ST[:, 0:256], kd[:, 0, :], v_nat[:, 0:256], start=True, stop=False)
                pe.matmul(ST[:, 0:256], kd[:, 1, :], v_nat[:, 256:512], start=False, stop=True)
                pe.wait_ge(diag_ready, h + 1)
                spread_v(0, TR)
                spread_v(1, TV).then_inc(step_b, 1)

            def c0_step(g):
                pe.wait_ge(s_new, 4 * g + 2)
                spread_v(2, TR)
                spread_v(3, TV).then_inc(step_c0, 1)

            def c1_step(g):
                pe.wait_ge(s_new, 4 * g + 4)
                pe.wait_ge(qpad_ready, g + 1)
                for b in range(TS):
                    j, i = b % 4, b // 4
                    mm = pe.matmul(SC[32 * j:32 * j + 32, 256 * i:256 * i + 256], qpad[:, b, :], s_t[:, b, :],
                                   start=True, stop=True, tile_position=(0, 32 * j))
                mm.then_inc(step_c1, 1)

            def d_step(g):
                pe.wait_ge(os_ready, g + 1)
                pe.wait_ge(sp_ready, g + 1)
                for n in range(4):
                    mm = pe.matmul(ST[:, 4 * n:4 * n + 4], scm[:, 128 * n:128 * n + 128], ident[:, 0:128:32],
                                   start=True, stop=True)
                mm.then_inc(step_d, 1)

            def e_step(g):
                pe.wait_ge(osum_ready, g + 1)
                pe.matmul(SC[:, 0:NT], ones[:, :], osum[:, :], start=True, stop=True).then_inc(step_e, 1)

            def f_step(g):
                pe.wait_ge(sqs_ready, g + 1)
                pe.matmul(O0[:, 0:NT], ones[:, :], osum[:, :], start=True, stop=True).then_inc(step_f, 1)

            def head(h, first=False):
                for c in range(6):
                    if not (first and c < 2):
                        project(h, c, h_hi, h_lo)
                    if not first:
                        (c0_step, c1_step, d_step, e_step, f_step, lambda g: None)[c](h - 1)
                    if c == 4:
                        a_step(h)
                    if c == 5:
                        b_step(h)

            pe.wait_ge(const_ready, 3)
            head(0, first=True)
            with pe.Fori(1, H) as h:
                head(h)

            for g in range(4):
                for r in range(4):
                    project(8, 4 * g + r, h_hi, h_lo)
                    if g == 0:
                        (c0_step, c1_step, d_step, e_step)[r](H - 1)
                    if g == 1 and r == 0:
                        f_step(H - 1)
                pe.wait_ge(pooled_ready, 3 * g + 3)
                pe.wait_ge(poolw_in, 16 * g + 16)
                if g >= 1:
                    pe.wait_ge(yaf_ready, 2 * g)
                for t, bank in enumerate((O1, TR)):
                    for k in range(2):
                        mm = pe.matmul(bank[:, 0:NT], pool_w[:, 256 * k + 128 * t:256 * k + 128 * t + 128],
                                       pooled[:, k, :], start=(k == 0), stop=(k == 1))
                mm.then_inc(pool_mm, 1)

            pe.wait_ge(yalo_ready, 3)
            for u in range(8):
                project(8, 16 + u, ya_hi, ya_lo, depth=8, parts=2, last=(6, yalo_ready, 4) if u == 0 else None)

            pe.wait_ge(ylo_ready, H)
            pe.wait_ge(yaf_ready, 8)

            def merge(it, first=False):
                a = 12 + it
                for c in range(6):
                    if c % 3 < 2:
                        project(a, c, h_hi, h_lo, after_ya=True)
                    else:
                        project(a, c, yb_hi, yb_lo, after_ya=True)
                    if c in (1, 3):
                        s = (c - 1) // 2
                        pe.wait_ge(gate_loaded[s], 16 * it + 16)
                        if s == 0 and not first:
                            pe.wait_ge(gpart_ready, it)
                        ada_unit(TR, gate_ring[:, s, :], s).then_inc(gate_used, 1)
                    if c == 5:
                        pe.wait_ge(gpart_ready, it + 1)
                        if not first:
                            pe.wait_ge(gbias_ready, it)
                        select(SC, 0).then_inc(gsel_done, 1)

            merge(0, first=True)
            with pe.Fori(1, 8) as it:
                merge(it)

            pe.wait_ge(mlo_ready, KT - 1)
            for c in range(6):
                project(20, c, m_hi, m_lo, last=(KT - 1, mlo_ready, KT) if c == 0 else None)
            for c in range(6):
                project(21, c, m_hi, m_lo)
            for c in range(4):
                project(22, c, m_hi, m_lo)
            pe.wait_ge(out_acc, KT)
            pe.matmul(O0[:, 0:NT], ones[:, :], sig_b[:, :], start=True, stop=True).then_inc(out_ms, 1)

        @block.scalar
        def _(act):
            def split(a, c, after_ya=False):
                i = 6 * a + c
                act.wait_ge(raw_loaded[c % 3], 16 * (2 * a + c // 3) + 16)
                if not isinstance(a, int):
                    act.wait_ge(proj_done, outs(a, c - 3, after_ya))
                elif i >= 3:
                    act.wait_ge(proj_done, outs(0, i - 3))
                act.activation(w_hi[:, c % 3, :], raw[:, c % 3, :], ACT.Copy).then_inc(hi_ready, 1)

            act.wait_ge(const_in, 80)
            act.wait_ge(c_zero, 1)
            act.activation(cpad[:, :, 0:NC], c_in[:, :, :], ACT.Silu).then_inc(c_ready, 1)
            act.wait_ge(const_ready, 2)
            act.activation(ones_r[:, :], ones[:, :], ACT.Copy).then_inc(const_ready, 1)
            act.wait_ge(x_in, 16)
            for n in range(KT // 2):
                if n >= 2:
                    act.wait_ge(x_sum, n - 1)
                act.activation((sq_t, bg_t)[n % 2][:, :, :], x_t[:, 2 * n:2 * n + 2, :], ACT.Square).then_inc(x_sq, 1)

            def ada_copy(p):
                for kind in range(2):
                    act.wait_ge(ada_used, 4 * p + 2 * kind + 2)
                    if not (isinstance(p, int) and p == 0):
                        act.wait_ge(sel_done, 2 * p - 1 + kind)
                    act.activation(part[:, kind, :], (TR, TV)[kind][:, 0:AW], ACT.Copy).then_inc(part_ready, 1)

            def split_h(p):
                act.wait_ge(hf_ready, 4 * p + 4)
                act.activation(h_hi[:, bass.ds(2 * p, 2), :], h_f[:, :, :], ACT.Copy).then_inc(h_hi_ready, 1)

            act.wait_ge(x_ms, 1)
            act.activation(rstd[:, :], O0[:, 0:NT], ACT.Sqrt, bias=eps_t[:, :], scale=1.0 / D_MODEL).then_inc(x_std, 1)
            split(0, 0)
            ada_copy(0)
            split_h(0)
            with act.Fori(1, 7) as p:
                ada_copy(p)
                split_h(p)
            split(0, 1)
            ada_copy(7)
            split_h(7)
            split(0, 2)

            def evac_qk(h, c):
                act.wait_ge(proj_done, 6 * h + c + 1)
                if not (isinstance(h, int) and 2 * h + c == 0):
                    act.wait_ge(rotated, 2 * h + c)
                bank = P[c % 2]
                act.activation(q_raw, bank[:, 0:NT], ACT.Copy)
                act.activation(work[0:64, 1, 0:NT], bank[64:128, 0:NT], ACT.Copy)
                act.activation(work[64:128, 1, 0:NT], bank[0:64, 0:NT], ACT.Copy).then_inc(taken, 1)

            def evac_v(h, t):
                act.wait_ge(proj_done, 6 * h + t + 3)
                if not (isinstance(h, int) and h == 0):
                    act.wait_ge(step_a, h)
                    act.wait_ge(vs_lo_ready, h)
                for u in range(2):
                    for half in range(2):
                        act.activation(v_blocks[64 * half:64 * half + 64, 2 * t + u, :], P[t][64 * u:64 * u + 64, TP:NT], ACT.Copy)
                act.activation(v_t[:, t, :], P[t][:, 0:NT], ACT.Copy).then_inc(taken, 1)

            def samples_v_hi(h):
                act.wait_ge(taken, 6 * h + 4)
                if not (isinstance(h, int) and h == 0):
                    act.wait_ge(diag_ready, h)
                act.activation(v_parts[:, :, :], v_blocks[:, :, :], ACT.Copy).then_inc(vs_hi_ready, 1)

            def evac_bg(h, t):
                act.wait_ge(proj_done, 6 * h + t + 5)
                if not (isinstance(h, int) and h == 0):
                    act.wait_ge(yf_ready, 2 * h)
                act.activation(bg_t[:, t, :], P[t][:, 0:NT], ACT.Silu).then_inc(taken, 1)

            def evac_os(g):
                act.wait_ge(step_c1, g + 1)
                act.activation(scm[:, :], SC[:, :], ACT.Copy).then_inc(os_ready, 1)

            def square_root(g):
                act.wait_ge(step_f, g + 1)
                act.activation(rstd[:, :], O0[:, 0:NT], ACT.Sqrt, bias=eps_t[:, :], scale=1.0 / DV).then_inc(std_ready, 1)

            def y_hi(g):
                act.wait_ge(yf_ready, 2 * g + 2)
                act.activation(yb_hi[:, bass.ds(2 * g, 2), :], o_t[:, :, :], ACT.Copy).then_inc(yhi_ready, 1)

            def evac_b(h):
                act.wait_ge(step_b, h + 1)
                if not (isinstance(h, int) and h == 0):
                    act.wait_ge(ylo_ready, h)
                    act.wait_ge(sp_out, 16 * h)
                act.activation(o_t[:, 0, 0:TP], O0[:, 0:TP], ACT.Copy).then_inc(o_ready, 1)
                act.activation(o_t[:, 1, 0:TP], O1[:, 0:TP], ACT.Copy).then_inc(o_ready, 1)
                act.activation(sp_t[:, :], ST[:, 0:DV], ACT.Copy).then_inc(sp_ready, 1)

            def head(h, first=False):
                evac_qk(h, 0)
                split(h, 3)
                evac_qk(h, 1)
                if not first:
                    evac_os(h - 1)
                split(h, 4)
                evac_v(h, 0)
                split(h, 5)
                evac_v(h, 1)
                samples_v_hi(h)
                split(h, 6)
                if not first:
                    square_root(h - 1)
                split(h, 7)
                act.wait_ge(step_a, h + 1)
                if not first:
                    act.wait_ge(step_b, h)
                act.activation(v_nat[:, :], TV[:, :], ACT.Copy).then_inc(vnat_ready, 1)
                if not first:
                    y_hi(h - 1)
                evac_bg(h, 0)
                act.wait_ge(state_in, 16 * h + 16)
                act.wait_ge(head_in, 16 * h + 16)
                act.activation(s_t[:, :, :], s_t[:, :, :], ACT.Copy, scale=hc[:, HC_GAMMA:HC_GAMMA + 1]).then_inc(s_scaled, 1)
                evac_bg(h, 1)
                evac_b(h)
                split(h, 8)

            head(0, first=True)
            with act.Fori(1, H) as h:
                head(h)

            for g in range(4):
                for t in range(2):
                    act.wait_ge(proj_done, 49 + 4 * g + t)
                    if g >= 1:
                        act.wait_ge(npool_ready, g)
                        act.wait_ge(pooled_ready, 3 * g)
                    else:
                        act.wait_ge(const_ready, 3)
                    act.activation(ext[:, t, 16:16 + TP], P[t][:, 0:TP], ACT.Copy)
                    act.activation(exts[:, t, :, 15], P[t][:, TP:NT], ACT.Copy).then_inc(taken, 1)
                    if g == 0 and t == 1:
                        evac_os(H - 1)
                    if g == 1 and t == 0:
                        square_root(H - 1)
                    split(8, 4 * g + t + 3)
                if g == 1:
                    y_hi(H - 1)
                if g >= 1:
                    act.wait_ge(yaf_ready, 2 * g)
                    act.activation(ya_hi[:, 2 * g - 2:2 * g, :], ya_f[:, :, :], ACT.Copy).then_inc(yahi_ready, 1)
                for t in range(2):
                    act.wait_ge(proj_done, 51 + 4 * g + t)
                    if g == 0:
                        act.wait_ge(s_new, 4 * H)
                        act.wait_ge(qpad_ready, H)
                    else:
                        act.wait_ge(yaf_ready, 2 * g)
                    act.activation(sil_a[:, t, :], P[t][:, 0:NT], ACT.Silu).then_inc(taken, 1)
                    split(8, 4 * g + t + 5)
            act.wait_ge(yaf_ready, 8)
            act.activation(ya_hi[:, 6:8, :], ya_f[:, :, :], ACT.Copy).then_inc(yahi_ready, 1)

            act.wait_ge(ylo_ready, H)
            act.wait_ge(yalo_ready, 4)
            act.wait_ge(state_out, 16 * H)
            act.wait_ge(sp_out, 16 * H)
            act.wait_ge(spool_out, 64)
            act.wait_ge(ppool_out, 16)
            for u in range(8):
                for t in range(2):
                    n = 2 * u + t
                    act.wait_ge(proj_done, 65 + n)
                    act.activation(ya_out[:, n, :], P[t][:, 0:NT], ACT.Copy).then_inc(taken, 1)
                split(8, 19 + u)

            def merge_hi(n):
                act.wait_ge(mf_ready, n + 1)
                act.activation(m_hi[:, bass.ds(n, 1), :], m_f[:, :].unsqueeze(1), ACT.Copy).then_inc(mhi_ready, 1)

            def merge(it, first=False):
                a = 12 + it
                for c in range(6):
                    j, n = c % 3, 2 * it + c // 3
                    act.wait_ge(proj_done, 81 + 6 * it + c)
                    if not (first and c < 3):
                        act.wait_ge(mf_ready, n)
                    bank = P[c % 2][:, 0:NT]
                    if j == 0:
                        act.activation(sig_a[:, :], bank, ACT.Sigmoid, bias=vecs[:, bass.ds(V_BMERGE + n, 1)]).then_inc(taken, 1)
                    elif j == 1:
                        act.activation(sig_b[:, :], bank, ACT.Sigmoid, bias=vecs[:, bass.ds(V_BMERGE + 16 + n, 1)]).then_inc(taken, 1)
                    else:
                        act.activation(yb_out[:, :], bank, ACT.Copy).then_inc(taken, 1)
                    if j == 0 and not (first and c == 0):
                        merge_hi(n - 1)
                    split(a, c + 3, after_ya=True)
                    if c == 4:
                        act.wait_ge(gate_used, 2 * it + 2)
                        act.activation(part[:, 0, :], TR[:, 0:AW], ACT.Copy).then_inc(gpart_ready, 1)

            merge(0, first=True)
            with act.Fori(1, 8) as it:
                merge(it)

            merge_hi(KT - 1)
            act.activation(eps_sqrt[:, :], eps_t[:, :], ACT.Sqrt)

            def out_tile(a, n, c):
                act.wait_ge(proj_done, 129 + n)
                act.activation(ya_out[:, bass.ds(n, 1), :], P[c % 2][:, 0:NT].unsqueeze(1), ACT.Copy).then_inc(taken, 1)
                if isinstance(a, int) and 6 * a + c + 3 >= 136:
                    return
                split(a, c + 3, after_ya=True)

            with act.Fori(0, 2) as m:
                for c in range(6):
                    out_tile(20 + m, 6 * m + c, c)
            for c in range(4):
                out_tile(22, 12 + c, c)
            act.wait_ge(out_ms, 1)
            act.activation(sig_a[:, :], O0[:, 0:NT], ACT.Sqrt, bias=eps_t[:, :], scale=1.0 / D_MODEL).then_inc(out_std, 1)

        @block.gpsimd
        def _(pool):
            def spread(h):
                v = v_parts[:, :, :].bitcast(f32).rearrange("p q b -> p b q").unsqueeze(3)
                pool.tensor_tensor(diag[:, :, :, :], ident2[:, :].unsqueeze(1).unsqueeze(1).to_broadcast([128, TS, 4, 64]),
                                   v.to_broadcast([128, TS, 4, 64]), ALU.mult).then_inc(diag_ready, 1)

            def squares(g):
                pool.wait_ge(cen_ready, 2 * g + 2)
                pool.tensor_tensor(sq_t[:, :, :], o_t[:, :, :], o_t[:, :, :], ALU.mult).then_inc(sq_ready, 1)
                pool.wait_ge(sq_ready, g + 1)
                pool.tensor_tensor(osum[:, :], sq_t[:, 0, :], sq_t[:, 1, :], ALU.add).then_inc(sqs_ready, 1)

            def head(h, first=False):
                if not first:
                    squares(h - 1)
                    pool.wait_ge(step_c0, h)
                pool.wait_ge(vs_lo_ready, h + 1)
                spread(h)

            pool.wait_ge(const_in, 80)
            head(0, first=True)
            with pool.Fori(1, H) as h:
                head(h)

            def windows(g):
                pool.wait_ge(taken, 50 + 4 * g)
                if g >= 1:
                    pool.wait_ge(pooled_ready, 3 * g)
                src, steps = ext, (1, 2, 4, 8)[:g + 1]
                for n, s in enumerate(steps):
                    dst = work[:, 2 * (n % 2):2 * (n % 2) + 2, :]
                    lo = 2 * s - 1
                    if n:
                        pool.wait_ge(win_step, sum(range(1, g + 1)) + n)
                    ins = pool.tensor_tensor(dst[:, :, lo:16 + TP], src[:, :, lo:16 + TP], src[:, :, lo - s:16 + TP - s], ALU.add)
                    ins.then_inc(win_step, 1)
                    src = dst

            windows(0)
            squares(H - 1)
            for g in range(1, 4):
                windows(g)

            pool.wait_ge(out_rstd, 1)
            pool.wait_ge(out_gated, 2 * KT)
            pool.wait_ge(x_again, 16)
            for q, (k0, k1) in enumerate(Y_POOL):
                y = ya_out[:, k0:k1, :]
                pool.tensor_tensor(y, y, yb_out[:, :].unsqueeze(1).to_broadcast([128, k1 - k0, NT]), ALU.mult).then_inc(y_scaled_p, 1)
                pool.wait_ge(y_scaled_p, q + 1)
                pool.tensor_tensor(y, y, x_late[:, k0:k1, :], ALU.add).then_inc(y_ready_p, 1)

        @block.vector
        def _(dve):
            def split(a, c, after_ya=False):
                i = 6 * a + c
                dve.wait_ge(hi_ready, i + 1)
                if not isinstance(a, int):
                    dve.wait_ge(proj_done, outs(a, c - 2, after_ya))
                elif i >= 2:
                    dve.wait_ge(proj_done, outs(0, i - 2))
                dve.tensor_tensor(w_lo[:, c % 2, :], raw[:, c % 3, :], w_hi[:, c % 3, :].bitcast(f32), ALU.subtract).then_inc(lo_ready, 1)

            dve.memset(cpad[:, :, :], 0.0).then_inc(c_zero, 1)
            dve.memset(eps_t[:, :], EPS)
            dve.memset(ones[:, :], 1.0).then_inc(const_ready, 1)
            dve.memset(ext[:, :, 0:16], 0.0)
            dve.memset(qpad[:, :, :], 0.0).then_inc(const_ready, 1)
            for n in range(KT // 2):
                dve.wait_ge(x_sq, n + 1)
                pair = (sq_t, bg_t)[n % 2]
                if n == 0:
                    dve.tensor_tensor(osum[:, :], pair[:, 0, :], pair[:, 1, :], ALU.add).then_inc(x_sum, 1)
                else:
                    dve.tensor_tensor(pair[:, 0, :], pair[:, 0, :], pair[:, 1, :], ALU.add).then_inc(hs_mul, 1)
                    dve.wait_ge(hs_mul, n)
                    dve.wait_ge(x_sum, n)
                    dve.tensor_tensor(osum[:, :], osum[:, :], pair[:, 0, :], ALU.add).then_inc(x_sum, 1)
            dve.wait_ge(x_std, 1)
            dve.reciprocal(rstd[:, :], rstd[:, :]).then_inc(x_rstd, 1)
            dve.wait_ge(x_rstd, 1)
            for k in range(KT):
                ins = dve.scalar_tensor_tensor(out=x_t[:, k, :], in0=x_t[:, k, :], scalar=vecs[:, V_GPRE + k:V_GPRE + k + 1],
                                               in1=rstd[:, :], op0=ALU.mult, op1=ALU.mult)
                ins.then_inc(xn_ready, 1)

            HM = KT // 2 - 1

            def make_h(p):
                first = isinstance(p, int) and p == 0
                dve.wait_ge(sel_done, 2 * p + 2)
                if not first:
                    dve.wait_ge(hf_ready, 4 * p)
                for kind, mod in enumerate((mod_scale, mod_shift)):
                    at = V_ADAB + (16 if kind == 0 else 0)
                    bias = vecs[:, bass.ds(2 * p + at, 2)].unsqueeze(2).to_broadcast([128, 2, NC])
                    got = SC[:, 32 * kind:32 * kind + 32].rearrange("p (t n) -> p t n", t=2)[:, :, 0:NC]
                    dve.scalar_tensor_tensor(out=mod[:, :, :], in0=got, scalar=1.0 - kind, in1=bias,
                                             op0=ALU.add, op1=ALU.add).then_inc(mod_ready, 1)
                dve.wait_ge(mod_ready, 2 * p + 2)
                dve.wait_ge(xn_ready, KT)
                if not first:
                    dve.wait_ge(h_lo_ready, p)
                    dve.wait_ge(h_hi_ready, p)
                for t in range(2):
                    dve.tensor_scalar(h_f[:, t, 0:TP].unsqueeze(1), x_t[:, bass.ds(2 * p + t, 1), 0:TP], mod_scale[:, t, 0:1], mod_shift[:, t, 0:1],
                                      ALU.mult, ALU.add).then_inc(hf_ready, 1)
                dve.tensor_tensor(h_f[:, :, TP:NT], x_t[:, bass.ds(2 * p, 2), TP:NT], mod_scale[:, :, 1:NC], ALU.mult).then_inc(hf_ready, 1)
                dve.wait_ge(hf_ready, 4 * p + 3)
                dve.tensor_tensor(h_f[:, :, TP:NT], h_f[:, :, TP:NT], mod_shift[:, :, 1:NC], ALU.add).then_inc(hf_ready, 1)
                dve.wait_ge(h_hi_ready, p + 1)
                dve.tensor_tensor(h_lo[:, bass.ds(2 * p, 2), :], h_f[:, :, :], h_hi[:, bass.ds(2 * p, 2), :].bitcast(f32),
                                  ALU.subtract).then_inc(h_lo_ready, 1)

            make_h(0)
            split(0, 0)
            with dve.Fori(1, 7) as p:
                make_h(p)
            split(0, 1)
            make_h(7)
            dve.wait_ge(trig_in, 32)

            def rotate(h, c):
                n = 2 * h + c
                dve.wait_ge(taken, 6 * h + c + 1)
                scale = 1.0 if c == 0 else DK ** -0.5
                if not (isinstance(h, int) and h == 0):
                    dve.wait_ge(step_a, h)
                dve.scalar_tensor_tensor(out=q_cos, in0=q_raw, scalar=scale, in1=trig_t[:, 0, :],
                                         op0=ALU.mult, op1=ALU.mult).then_inc(rot_mul, 1)
                dve.scalar_tensor_tensor(out=q_swap, in0=q_swap, scalar=scale, in1=trig_t[:, 1, :],
                                         op0=ALU.mult, op1=ALU.mult).then_inc(rot_mul, 1)
                dve.wait_ge(rot_mul, 2 * n + 2)
                dve.tensor_tensor(qk_t[:, c, :], q_cos, q_swap, ALU.add).then_inc(rotated, 1)

            def pad_q(h):
                dve.wait_ge(rotated, 2 * h + 1)
                if not (isinstance(h, int) and h == 0):
                    dve.wait_ge(step_c1, h)
                dve.tensor_copy(qpad[:, :, 0], qk_t[:, 0, TP:NT]).then_inc(qpad_ready, 1)

            def update_state(h, half):
                dve.wait_ge((step_b, step_c0)[half], h + 1)
                if half == 0:
                    dve.wait_ge(s_scaled, h + 1)
                for n, bank in enumerate((TR, TV)):
                    for m in range(2):
                        b = 4 * half + 2 * n + m
                        ins = dve.scalar_tensor_tensor(out=s_t[:, b, :], in0=bank[:, 256 * m:256 * m + 256], scalar=qk_t[:, 1, TP + b:TP + b + 1],
                                                       in1=s_t[:, b, :], op0=ALU.mult, op1=ALU.add)
                    ins.then_inc(s_new, 1)

            def collect(g):
                dve.wait_ge(step_d, g + 1)
                dve.wait_ge(o_ready, 2 * g + 2)
                src = ST[:, 0:16].rearrange("p (i t j) -> p t i j", i=2, t=2)
                dst = o_t[:, :, TP:NT].rearrange("p t (i j) -> p t i j", i=2)
                dve.tensor_copy(dst, src).then_inc(o_samples, 1)
                dve.wait_ge(o_samples, g + 1)
                if not (isinstance(g, int) and g == 0):
                    dve.wait_ge(step_f, g)
                dve.tensor_tensor(osum[:, :], o_t[:, 0, :], o_t[:, 1, :], ALU.add).then_inc(osum_ready, 1)

            def centre(g):
                dve.wait_ge(step_e, g + 1)
                for t in range(2):
                    dve.scalar_tensor_tensor(out=o_t[:, t, :], in0=SC[:, 0:NT], scalar=-1.0 / DV, in1=o_t[:, t, :],
                                             op0=ALU.mult, op1=ALU.add).then_inc(cen_ready, 1)

            def norm(g):
                dve.wait_ge(std_ready, g + 1)
                dve.wait_ge(sqs_ready, g + 1)
                dve.reciprocal(rstd[:, :], rstd[:, :]).then_inc(rstd_ready, 1)
                dve.wait_ge(rstd_ready, g + 1)
                dve.wait_ge(taken, 6 * g + 6)
                for t in range(2):
                    dve.scalar_tensor_tensor(out=o_t[:, t, :], in0=o_t[:, t, :], scalar=gn_cur[:, t:t + 1], in1=rstd[:, :],
                                             op0=ALU.mult, op1=ALU.mult).then_inc(ynorm_ready, 1)
                dve.wait_ge(ynorm_ready, 2 * g + 2)
                for t in range(2):
                    dve.tensor_tensor(o_t[:, t, :], o_t[:, t, :], bg_t[:, t, :], ALU.mult).then_inc(yf_ready, 1)

            def y_lo(g):
                dve.wait_ge(yhi_ready, g + 1)
                dve.tensor_tensor(yb_lo[:, bass.ds(2 * g, 2), :], o_t[:, :, :], yb_hi[:, bass.ds(2 * g, 2), :].bitcast(f32),
                                  ALU.subtract).then_inc(ylo_ready, 1)

            def decay(h):
                dve.wait_ge(step_a, h + 1)
                dve.wait_ge(head_in, 16 * h + 16)
                if not (isinstance(h, int) and h == 0):
                    dve.wait_ge(step_b, h)
                    dve.wait_ge(step_d, h)
                dve.tensor_tensor(scm[:, 0:256], SC[:, 0:256], hc[:, 0:256], ALU.mult).then_inc(scm_ready, 1)
                dve.tensor_tensor(scm[:, 256:384], SC[:, 256:384], hc[:, 0:128], ALU.mult).then_inc(scm_ready, 1)
                for c in range(2):
                    dve.tensor_scalar(kd[:, c, :], TR[:, 128 * c:128 * c + 128], hc[:, HC_KD0 + c:HC_KD0 + c + 1], None,
                                      ALU.mult).then_inc(kd_ready, 1)

            def head(h, first=False):
                rotate(h, 0)
                if not first:
                    update_state(h - 1, 1)
                split(h, 2)
                rotate(h, 1)
                pad_q(h)
                split(h, 3)
                if not first:
                    collect(h - 1)
                split(h, 4)
                dve.wait_ge(vs_hi_ready, h + 1)
                dve.tensor_tensor(v_parts[64:128, :, :], v_blocks[64:128, :, :], v_parts[64:128, :, :].bitcast(f32),
                                  ALU.subtract).then_inc(vs_lo_ready, 1)
                if not first:
                    centre(h - 1)
                split(h, 5)
                if not first:
                    norm(h - 1)
                decay(h)
                if not first:
                    y_lo(h - 1)
                split(h, 6)
                dve.tensor_copy(gn_cur[:, :], hc[:, HC_GN:HC_GN + 2]).then_inc(gn_saved, 1)
                update_state(h, 0)
                split(h, 7)

            head(0, first=True)
            with dve.Fori(1, H) as h:
                head(h)

            def split_ya(g):
                dve.wait_ge(yahi_ready, g + 1)
                dve.tensor_tensor(ya_lo[:, 2 * g:2 * g + 2, :], ya_f[:, :, :], ya_hi[:, 2 * g:2 * g + 2, :].bitcast(f32),
                                  ALU.subtract).then_inc(yalo_ready, 1)

            update_state(H - 1, 1)
            for g in range(4):
                w = WINDOWS[g]
                split(8, 4 * g + 2)
                if g == 1:
                    norm(H - 1)
                dve.wait_ge(spool_in, 16 * g + 16)
                if g >= 1:
                    dve.wait_ge(npool_ready, g)
                dve.tensor_copy(exts[:, :, :, 0:15], sp_in[:, :, :, :]).then_inc(exts_old, 1)
                split(8, 4 * g + 3)
                if g == 0:
                    collect(H - 1)
                else:
                    split_ya(g - 1)
                if g == 1:
                    y_lo(H - 1)
                dve.wait_ge(taken, 50 + 4 * g)
                dve.wait_ge(exts_old, g + 1)
                if g == 0:
                    dve.wait_ge(step_a, H)
                else:
                    dve.wait_ge(pool_mm, g)
                    dve.wait_ge(spool_out, 16 * g)
                dve.tensor_reduce(win_s[:, :, :], exts[:, :, :, 16 - w:16], AX.X, ALU.add).then_inc(wins_ready, 1)
                dve.tensor_copy(npp_t[:, 2 * g:2 * g + 2, :], ext[:, :, 16 + TP - 15:16 + TP]).then_inc(ppool_ready, 1)
                dve.wait_ge(win_step, sum(range(1, g + 2)))
                win = work[:, 2 * (g % 2):2 * (g % 2) + 2, :]
                dve.scalar_tensor_tensor(out=pooled[:, :, 16:TP], in0=win[:, :, 32:16 + TP], scalar=1.0 / w,
                                         in1=ext[:, :, 32:16 + TP], op0=ALU.mult, op1=ALU.subtract).then_inc(pooled_ready, 1)
                count = cnt_t[:, g:g + 1, :].to_broadcast([128, 2, 16])
                dve.tensor_tensor(win[:, :, 16:32], win[:, :, 16:32], count, ALU.mult).then_inc(head_cols, 1)
                dve.wait_ge(head_cols, g + 1)
                dve.tensor_tensor(pooled[:, :, 0:16], win[:, :, 16:32], ext[:, :, 16:32], ALU.subtract).then_inc(pooled_ready, 1)
                dve.wait_ge(wins_ready, g + 1)
                dve.scalar_tensor_tensor(out=pooled[:, :, TP:NT], in0=win_s[:, :, :], scalar=1.0 / w, in1=exts[:, :, :, 15],
                                         op0=ALU.mult, op1=ALU.subtract).then_inc(pooled_ready, 1)
                dve.tensor_copy(nps_t[:, :, :, :], exts[:, :, :, 1:16]).then_inc(npool_ready, 1)
                split(8, 4 * g + 4)
                if g == 0:
                    centre(H - 1)
                split(8, 4 * g + 5)
                dve.wait_ge(pool_mm, g + 1)
                dve.wait_ge(taken, 52 + 4 * g)
                if g >= 1:
                    dve.wait_ge(yalo_ready, g)
                for t, bank in enumerate((O1, TR)):
                    dve.scalar_tensor_tensor(out=ya_f[:, t, :], in0=bank[:, 0:NT], scalar=vecs[:, V_PSCALE + 2 * g + t:V_PSCALE + 2 * g + t + 1],
                                             in1=sil_a[:, t, :], op0=ALU.mult, op1=ALU.mult).then_inc(yaf_ready, 1)
            split_ya(3)

            for u in range(8):
                split(8, 18 + u)

            def merge_lo(n):
                dve.wait_ge(mhi_ready, n + 1)
                dve.tensor_tensor(m_lo[:, bass.ds(n, 1), :], m_f[:, :].unsqueeze(1), m_hi[:, bass.ds(n, 1), :].bitcast(f32),
                                  ALU.subtract).then_inc(mlo_ready, 1)

            def merge(it, first=False):
                a = 12 + it
                for c in range(6):
                    if c % 3 == 2:
                        n = 2 * it + c // 3
                        dve.wait_ge(taken, 81 + 6 * it + c)
                        if not (first and c == 2):
                            dve.wait_ge(mlo_ready, n)
                        dve.tensor_tensor(sig_a[:, :].unsqueeze(1), sig_a[:, :].unsqueeze(1), ya_out[:, bass.ds(n, 1), :], ALU.mult).then_inc(merge_mul, 1)
                        dve.tensor_tensor(sig_b[:, :], sig_b[:, :], yb_out[:, :], ALU.mult).then_inc(merge_mul, 1)
                        dve.wait_ge(merge_mul, 2 * n + 2)
                        dve.tensor_tensor(m_f[:, :], sig_a[:, :], sig_b[:, :], ALU.add).then_inc(mf_ready, 1)
                    split(a, c + 2, after_ya=True)
                    if c % 3 == 0 and not (first and c == 0):
                        merge_lo(2 * it + c // 3 - 1)
                dve.wait_ge(gsel_done, it + 1)
                tiles = bass.ds(2 * it, 2)
                got = SC[:, 0:32].rearrange("p (t n) -> p t n", t=2)[:, :, 0:NC]
                bias = vecs[:, bass.ds(2 * it + V_ADAB + 32, 2)].unsqueeze(2).to_broadcast([128, 2, NC])
                post = vecs[:, bass.ds(2 * it + V_GPOST, 2)].unsqueeze(2).to_broadcast([128, 2, NC])
                dve.tensor_tensor(mod_scale[:, :, :], got, bias, ALU.add).then_inc(gbias_ready, 1)
                dve.wait_ge(gbias_ready, it + 1)
                dve.tensor_tensor(gate_g[:, tiles, :], mod_scale[:, :, :], post, ALU.mult).then_inc(gate_ready, 1)

            merge(0, first=True)
            with dve.Fori(1, 8) as it:
                merge(it)
            merge_lo(KT - 1)

            def out_tile(a, n, c, first=False):
                dve.wait_ge(taken, 129 + n)
                tile = bass.ds(n, 1)
                o = ya_out[:, tile, :]
                if not first:
                    dve.wait_ge(out_acc, n)
                dve.tensor_tensor(sig_a[:, :].unsqueeze(1), o, o, ALU.mult).then_inc(out_sq, 1)
                dve.wait_ge(out_sq, n + 1)
                if first:
                    dve.tensor_copy(sig_b[:, :], sig_a[:, :]).then_inc(out_acc, 1)
                else:
                    dve.tensor_tensor(sig_b[:, :], sig_b[:, :], sig_a[:, :], ALU.add).then_inc(out_acc, 1)
                dve.tensor_tensor(ya_out[:, tile, 0:TP], ya_out[:, tile, 0:TP], gate_g[:, tile, 0:1].to_broadcast([128, 1, TP]),
                                  ALU.mult).then_inc(out_gated, 1)
                dve.tensor_tensor(ya_out[:, tile, TP:NT], ya_out[:, tile, TP:NT], gate_g[:, tile, 1:NC], ALU.mult).then_inc(out_gated, 1)
                if isinstance(a, int) and 6 * a + c + 2 >= 136:
                    return
                split(a, c + 2, after_ya=True)

            dve.wait_ge(gate_ready, 8)
            out_tile(20, 0, 0, first=True)
            for c in range(1, 6):
                out_tile(20, c, c)
            for c in range(6):
                out_tile(21, 6 + c, c)
            for c in range(4):
                out_tile(22, 12 + c, c)
            dve.wait_ge(out_std, 1)
            dve.reciprocal(yb_out[:, :], sig_a[:, :]).then_inc(out_rstd, 1)
            dve.wait_ge(out_rstd, 1)
            dve.wait_ge(out_gated, 2 * KT)
            dve.wait_ge(x_again, 16)
            for q, (k0, k1) in enumerate(Y_DVE):
                y = ya_out[:, k0:k1, :]
                dve.tensor_tensor(y, y, yb_out[:, :].unsqueeze(1).to_broadcast([128, k1 - k0, NT]), ALU.mult).then_inc(y_scaled, 1)
                dve.wait_ge(y_scaled, q + 1)
                dve.tensor_tensor(y, y, x_late[:, k0:k1, :], ALU.add).then_inc(y_ready, 1)


def constants():
    f = np.float32
    m = np.arange(128)
    head = np.zeros((H, 128, TP + 3))
    for h in range(H):
        lg = np.log1p(-(2.0 ** (-5.0 - h)))
        d = np.arange(TP)[None, :] - m[:, None]
        head[h, :, 0:TP] = np.where(d >= 0, np.exp(np.maximum(d, 0) * lg), 0.0)
        head[h, :, HC_KD0] = np.exp((TP - 1 - m) * lg)
        head[h, :, HC_KD1] = np.exp((127 - m) * lg)
        head[h, :, HC_GAMMA] = np.exp(lg)
    half = DK // 2
    inv = (10000.0 ** (-np.arange(half, dtype=f) / f(half))).astype(f)
    pos = np.concatenate([np.arange(TP), np.full(TS, PAST_LEN)]).astype(f)
    ang = (pos[None, :] * inv[:, None]).astype(f).astype(np.float64)
    cos, sin = np.cos(ang), np.sin(ang)
    trig = np.stack([np.concatenate([cos, cos]), np.concatenate([-sin, sin])], axis=1)
    sel = np.zeros((128, NC))
    for j in range(4):
        sel[32 * j + np.arange(NC), np.arange(NC)] = 1.0
    cnt = np.stack([1.0 / np.minimum(np.arange(16) + 1, w) for w in WINDOWS])
    cnt = np.broadcast_to(cnt, (128, 4, 16))
    return head.astype(f), trig.astype(f), np.eye(128, dtype=f), sel.astype(f), np.ascontiguousarray(cnt, dtype=f)


def kernel(x_prompt, x_sample, state_pool, state_ret, c_prompt, c_sample, ada_w, ada_b, g_pre, g_post,
           w_in, pool_w, pool_scale, gn_g, w_a_proj, w_b_proj, w_merge, b_merge, w_out):
    import concourse.bacc as bacc
    from concourse.bass_utils import run_bass_kernel_spmd

    A = lambda x: np.asarray(x)
    tiles = lambda v: A(v).reshape(-1, 128).T
    feat = lambda m: m.reshape(m.shape[0], -1, 128).transpose(2, 1, 0)
    block = lambda w, c: w[:, c:c + 128].reshape(-1, 128, 128).transpose(1, 0, 2).reshape(128, -1)

    win, wm, wa, wb, wo = A(w_in)[0], A(w_merge)[0], A(w_a_proj)[0], A(w_b_proj)[0], A(w_out)[0]
    units = []
    Q0, K0, V0, B0 = 2 * D_POOL, 2 * D_POOL + H * DK, 2 * D_POOL + 2 * H * DK, 2 * D_POOL + 2 * H * DK + H * DV
    for h in range(H):
        for c in (Q0 + DK * h, K0 + DK * h, V0 + DV * h, V0 + DV * h + 128, B0 + DV * h, B0 + DV * h + 128):
            units.append(block(win, c))
    for g in range(4):
        for c in (256 * g, 256 * g + 128, D_POOL + 256 * g, D_POOL + 256 * g + 128):
            units.append(block(win, c))
    for u in range(8):
        units.append(np.concatenate([block(wa, 256 * u), block(wa, 256 * u + 128)], axis=1))
    for n in range(KT):
        units += [block(wm, 128 * n), block(wm, D_MODEL + 128 * n), block(wb, 128 * n)]
    for n in range(KT):
        units.append(block(wo, 128 * n))
    stream = np.stack(units)

    aw = A(ada_w)[0]

    def ada_units(c):
        w = aw[:, c:c + AW].reshape(2, 8, 128, AW).transpose(0, 2, 1, 3).reshape(2, 128, UNIT)
        return [w[0], w[1]]
    ada0 = np.stack([u for p in range(8) for c in (D_MODEL + AW * p, AW * p) for u in ada_units(c)])
    ada1 = np.stack([u for p in range(8) for u in ada_units(2 * D_MODEL + AW * p)])

    head, trig, ident, sel, cnt = constants()
    gn = A(gn_g)[0].reshape(H, 2, 128).transpose(0, 2, 1)
    ins = {
        "stream": stream, "ada0": ada0, "ada1": ada1,
        "xT": np.concatenate([feat(A(x_prompt)[0]), feat(A(x_sample)[:, 0])], axis=2),
        "cT": np.concatenate([feat(A(c_prompt)), feat(A(c_sample))], axis=2),
        "vec": np.concatenate([tiles(A(g_pre)[0]), tiles(A(g_post)[0]), tiles(A(ada_b)[0]), tiles(A(b_merge)[0]),
                               tiles(A(pool_scale)[0])], axis=1),
        "headc": np.concatenate([head, gn], axis=2), "trig": trig, "ident_in": ident, "ident2_in": ident[:, 0:64] + ident[:, 64:128], "sel_in": sel, "cnt_in": cnt,
        "poolw": A(pool_w)[0].reshape(4, 2, 128, 256).transpose(0, 2, 1, 3).reshape(4, 128, 512),
        "spool": A(state_pool)[0].reshape(TS, POOL_BUF, 4, 2, 128).transpose(2, 4, 3, 0, 1),
        "sret": A(state_ret)[0].transpose(1, 2, 0, 3),
    }
    outputs = {"yT": (128, KT, NT), "npool_p": (128, 8, POOL_BUF), "npool_s": (4, 128, 2, TS, POOL_BUF),
               "nret_p": (H, 128, DV), "nret_s": (H, 128, TS, DV)}
    nc = bacc.Bacc("TRN2", target_bir_lowering=False, num_devices=1)
    arrays, aps = {}, {}
    for name, a in ins.items():
        arrays[name] = np.ascontiguousarray(a)
        aps[name] = nc.dram_tensor(name, a.shape, mybir.dt.from_np(a.dtype), kind="ExternalInput").ap()
    for name, shape in outputs.items():
        aps[name] = nc.dram_tensor(name, shape, mybir.dt.float32, kind="ExternalOutput").ap()
    build(nc, **aps)
    r = run_bass_kernel_spmd(nc, [arrays], core_ids=[0]).results[0]
    y = r["yT"].transpose(2, 1, 0).reshape(NT, D_MODEL)
    return (y[:TP].reshape(1, TP, D_MODEL), y[TP:].reshape(TS, 1, D_MODEL),
            r["npool_p"].transpose(2, 1, 0).reshape(1, 1, POOL_BUF, D_POOL),
            r["nret_p"].reshape(1, 1, H, DK, DV),
            r["npool_s"].transpose(3, 4, 0, 2, 1).reshape(1, TS, POOL_BUF, D_POOL),
            r["nret_s"].transpose(2, 0, 1, 3).reshape(1, TS, H, DK, DV))
```

```python
import numpy as np
import concourse.bass as bass
from concourse import mybir
from contextlib import ExitStack

D_MODEL = 2048
TP = 256
TS = 8
NT = TP + TS
KT = D_MODEL // 128
NC = 1 + TS
D_POOL = D_MODEL // 2
WINDOWS = (2, 4, 8, 16)
POOL_BUF = max(WINDOWS) - 1
H = 8
DK = D_MODEL // 16
DV = D_MODEL // 8
PAST_LEN = 2048
EPS = 1e-6
UNIT = KT * 128
AW = 256
V_GPRE, V_GPOST, V_ADAB, V_BMERGE, V_PSCALE = 0, 16, 32, 80, 112
V_N = 120
HC_KD0, HC_KD1, HC_GAMMA, HC_GN = TP, TP + 1, TP + 2, TP + 3
HC_N = TP + 5
Y_DVE, Y_POOL = ((0, 2), (2, 5), (5, 8), (8, 10), (10, 11)), ((11, 14), (14, 16))
U3_FIRST = 4


def outs(a, c, after_ya=False):
    i = 6 * a + c
    if not isinstance(a, int):
        return i + (9 if after_ya else 1)
    return i + 1 if i < 64 else (64 + 2 * (i - 63) if i < 72 else i + 9)


def build(nc, stream, ada0, ada1, xT, cT, vec, headc, trig, ident_in, sel_in, cnt_in, poolw, spool,
          sret, yT, npool_p, npool_s, nret_p, nret_s, v_dram):
    f32, f32r = mybir.dt.float32, mybir.dt.float32r
    ALU, ACT, AX = mybir.AluOpType, mybir.ActivationFunctionType, mybir.AxisListType

    ctx = ExitStack()
    with ctx:
        def sb(name, shape, dt=f32, stack=ctx):
            return stack.enter_context(nc.sbuf_tensor(name, shape, dt))

        def sem(name):
            return ctx.enter_context(nc.semaphore(name))

        with ExitStack() as start:
            unit3_lo = sb("unit3_lo", [128, UNIT], f32r, start)
        raw = sb("raw", [128, 3, UNIT])
        w_hi = sb("w_hi", [128, 3, UNIT], f32r)
        w_lo = sb("w_lo", [128, 2, UNIT], f32r)
        h_hi = sb("h_hi", [128, KT, NT], f32r)
        h_lo = sb("h_lo", [128, KT, NT], f32r)
        cpad = sb("cpad", [128, KT, 32])
        c_in = sb("c_in", [128, KT, NC])
        part = sb("part", [128, 2, AW])
        vecs = sb("vecs", [128, V_N])
        ident = sb("ident", [128, 128])
        ones = sb("ones", [128, 128])
        sel = sb("sel", [128, NC])
        eps_t = sb("eps_t", [128, 1])
        eps_sqrt = sb("eps_sqrt", [128, 1])
        mod_scale = sb("mod_scale", [128, 2, NC])
        mod_shift = sb("mod_shift", [128, 2, NC])
        gate_g = sb("gate_g", [128, KT, NC])
        with ExitStack() as start:
            unit4 = sb("unit4", [128, 2, UNIT], f32r, start)
        early = ExitStack()
        ada_ring = sb("ada_ring", [128, 4, UNIT], f32, early)
        x_t = sb("x_t", [128, KT, NT], f32, early)
        early.close()
        yb_hi = sb("yb_hi", [128, KT, NT], f32r)
        yb_lo = sb("yb_lo", [128, KT, NT], f32r)
        mid = ExitStack()
        ya_hi = sb("ya_hi", [128, KT // 2, NT], f32r, mid)
        ya_lo = sb("ya_lo", [128, KT // 2, NT], f32r, mid)
        work = sb("work", [128, 4, 16 + TP], f32, mid)
        qk_t = sb("qk_t", [128, 2, NT], f32, mid)
        v_t = sb("v_t", [128, 2, NT], f32, mid)
        scm = sb("scm", [128, 512], f32, mid)
        v_nat = sb("v_nat", [128, 512], f32, mid)
        v_cen = sb("v_cen", [128, 2, DV], f32, mid)
        v_sum = sb("v_sum", [128, 2], f32, mid)
        v_mean = sb("v_mean", [128, 2], f32, mid)
        os_sum = sb("os_sum", [128, 2], f32, mid)
        os_mean = sb("os_mean", [128, 2], f32, mid)
        kd = sb("kd", [128, 2, 128], f32, mid)
        with ExitStack() as start:
            unit2_lo = sb("unit2_lo", [128, UNIT], f32r, start)
        v_all = sb("v_all", [128, DV // 2, 2, TS], f32, mid)
        with ExitStack() as start:
            unit3_hi = sb("unit3_hi", [128, UNIT], f32r, start)
        s_t = sb("s_t", [128, TS, DV], f32, mid)
        sp_t = sb("sp_t", [128, DV], f32, mid)
        o_t = sb("o_t", [128, 2, NT], f32, mid)
        sq_t = sb("sq_t", [128, 2, NT], f32, mid)
        osum = sb("osum", [128, NT], f32, mid)
        osum_hi = sb("osum_hi", [128, NT], f32r, mid)
        osum_lo = sb("osum_lo", [128, NT], f32r, mid)
        ones_r = sb("ones_r", [128, 128], f32r, mid)
        rstd = sb("rstd", [128, NT], f32, mid)
        bg_t = sb("bg_t", [128, 2, NT], f32, mid)
        qpad = sb("qpad", [128, TS, 32], f32, mid)
        trig_t = sb("trig_t", [128, 2, NT], f32, mid)
        hc = sb("hc", [128, HC_N], f32, mid)
        gn_cur = sb("gn_cur", [128, 2], f32, mid)
        ext = sb("ext", [128, 2, 16 + TP], f32, mid)
        exts = sb("exts", [128, 2, TS, 16], f32, mid)
        sp_in = sb("sp_in", [128, 2, TS, POOL_BUF], f32, mid)
        nps_t = sb("nps_t", [128, 2, TS, POOL_BUF], f32, mid)
        npp_t = sb("npp_t", [128, 8, POOL_BUF], f32, mid)
        cnt_t = sb("cnt_t", [128, 4, 16], f32, mid)
        win_s = sb("win_s", [128, 2, TS], f32, mid)
        mid.close()
        late = ExitStack()
        m_hi = sb("m_hi", [128, KT, NT], f32r, late)
        ya_out = sb("ya_out", [128, KT, NT], f32, late)
        m_lo = sb("m_lo", [128, KT, NT], f32r, late)
        gate_ring = sb("gate_ring", [128, 2, UNIT], f32, late)
        sig_a = sb("sig_a", [128, NT], f32, late)
        sig_b = sb("sig_b", [128, NT], f32, late)
        yb_out = sb("yb_out", [128, NT], f32, late)
        m_f = sb("m_f", [128, NT], f32, late)
        late.close()
        h_f = v_t
        q_raw, q_swap, q_cos = work[:, 0, 0:NT], work[:, 1, 0:NT], work[:, 2, 0:NT]
        pooled, pool_w, sil_a, ya_f = v_t, v_nat, qk_t, trig_t

        banks = [ctx.enter_context(nc.psum_tensor(f"bank{n}", [128, 512], f32)) for n in range(8)]
        P = banks[0:2]
        TR, TV, SC, O0, O1, ST = banks[2:8]

        const_in = sem("const_in")
        x_in = sem("x_in")
        trig_in = sem("trig_in")
        raw_loaded = [sem(f"raw_loaded{s}") for s in range(3)]
        hi_ready, lo_ready = sem("hi_ready"), sem("lo_ready")
        proj_done, taken = sem("proj_done"), sem("taken")
        ada_loaded = [sem(f"ada_loaded{s}") for s in range(4)]
        ada_used, part_ready, sel_done = sem("ada_used"), sem("part_ready"), sem("sel_done")
        mod_ready, hf_ready, h_hi_ready, h_lo_ready = sem("mod_ready"), sem("hf_ready"), sem("h_hi_ready"), sem("h_lo_ready")
        c_zero, c_ready, const_ready = sem("c_zero"), sem("c_ready"), sem("const_ready")
        x_sq, x_sum, x_ms, x_std, x_rstd, xn_ready = (sem("x_sq"), sem("x_sum"), sem("x_ms"), sem("x_std"),
                                                      sem("x_rstd"), sem("xn_ready"))
        hs_mul = sem("hs_mul")
        head_in, state_in, state_out, sp_out = sem("head_in"), sem("state_in"), sem("state_out"), sem("sp_out")
        rot_mul, rotated, qpad_ready = sem("rot_mul"), sem("rotated"), sem("qpad_ready")
        v_stored, v_spread = sem("v_stored"), sem("v_spread")
        step_a, step_b, step_c, step_d, step_e = (sem(f"step_{x}") for x in ("a", "b", "c", "d", "e"))
        vnat_ready, kd_ready, scm_ready = sem("vnat_ready"), sem("kd_ready"), sem("scm_ready")
        o_ready, sp_ready, s_scaled, s_new, os_ready = sem("o_ready"), sem("sp_ready"), sem("s_scaled"), sem("s_new"), sem("os_ready")
        vmean_ready, vcen_ready, osmean_ready, oscen_ready = (sem("vmean_ready"), sem("vcen_ready"), sem("osmean_ready"),
                                                              sem("oscen_ready"))
        o_samples, sq_ready, sqs_ready, sqhi_ready, sqlo_ready = (
            sem("o_samples"), sem("sq_ready"), sem("sqs_ready"), sem("sqhi_ready"), sem("sqlo_ready"))
        std_ready, rstd_ready, ynorm_ready, yf_ready, yhi_ready, ylo_ready, gn_saved = (
            sem("std_ready"), sem("rstd_ready"), sem("ynorm_ready"), sem("yf_ready"), sem("yhi_ready"), sem("ylo_ready"), sem("gn_saved"))
        spool_in, poolw_in, spool_out = sem("spool_in"), sem("poolw_in"), sem("spool_out")
        exts_old, win_step, wins_ready = sem("exts_old"), sem("win_step"), sem("wins_ready")
        head_cols, pooled_ready, pool_mm = sem("head_cols"), sem("pooled_ready"), sem("pool_mm")
        yaf_ready, yahi_ready, yalo_ready, npool_ready, ppool_ready, ppool_out = (
            sem("yaf_ready"), sem("yahi_ready"), sem("yalo_ready"), sem("npool_ready"), sem("ppool_ready"), sem("ppool_out"))
        gate_loaded = [sem(f"gate_loaded{s}") for s in range(2)]
        gate_used, gpart_ready, gsel_done, gbias_ready, gate_ready = (
            sem("gate_used"), sem("gpart_ready"), sem("gsel_done"), sem("gbias_ready"), sem("gate_ready"))
        merge_mul, mf_ready, mhi_ready, mlo_ready = (
            sem("merge_mul"), sem("mf_ready"), sem("mhi_ready"), sem("mlo_ready"))
        out_sq, out_acc, out_gated, last_sq, out_ms, out_std, out_rstd = (
            sem("out_sq"), sem("out_acc"), sem("out_gated"), sem("last_sq"), sem("out_ms"), sem("out_std"), sem("out_rstd"))
        x_again, y_scaled, y_ready, y_out = sem("x_again"), sem("y_scaled"), sem("y_ready"), sem("y_out")
        y_scaled_p, y_ready_p = sem("y_scaled_p"), sem("y_ready_p")
        EARLY_HI = [w_hi[:, 0, :], w_hi[:, 1, :], w_hi[:, 2, :], unit3_hi[:, :], unit4[:, 0, :]]
        EARLY_LO = [w_lo[:, 0, :], w_lo[:, 1, :], unit2_lo[:, :], unit3_lo[:, :],
                    unit4[:, 1, :]]
        EARLY_BANK = [P[0], P[1], O1, ST, P[0]]
        x_late = raw[:, :, :].rearrange("p s n -> p (s n)")[:, 0:KT * NT].rearrange("p (k t) -> p k t", k=KT)

        block = ctx.enter_context(nc.Block())

        @block.sync
        def _(sp):
            def load(a, c):
                i = 6 * a + c
                if not isinstance(a, int) or i >= 3:
                    sp.wait_ge(lo_ready, i - 2)
                if isinstance(a, int) and i == 6:
                    sp.wait_ge(proj_done, 4)
                sp.dma_start(raw[:, c % 3, :], stream[i]).then_inc(raw_loaded[c % 3], 16)

            sp.dma_start(x_t[:, :, :], xT).then_inc(x_in, 16)
            sp.dma_start(c_in[:, :, :], cT).then_inc(const_in, 16)
            sp.dma_start(vecs[:, :], vec).then_inc(const_in, 16)
            sp.dma_start(ident[:, :], ident_in).then_inc(const_in, 16)
            sp.dma_start(sel[:, :], sel_in).then_inc(const_in, 16)
            for s in range(4):
                sp.dma_start(ada_ring[:, s, :], ada0[s]).then_inc(ada_loaded[s], 16)
            load(0, 0)
            load(0, 1)

            def ada_load(p):
                for s in range(4):
                    sp.wait_ge(ada_used, 4 * p + s - 3)
                    sp.dma_start(ada_ring[:, s, :], ada0[4 * p + s]).then_inc(ada_loaded[s], 16)

            with sp.Fori(1, 6) as p:
                ada_load(p)
            load(0, 2)
            ada_load(6)
            load(0, 3)
            ada_load(7)
            load(0, 4)
            sp.dma_start(trig_t[:, :, :], trig).then_inc(trig_in, 16)
            sp.dma_start(cnt_t[:, :, :], cnt_in).then_inc(trig_in, 16)
            load(0, 5)
            sp.dma_start(hc[:, :], headc[0]).then_inc(head_in, 16)
            load(0, 6)
            load(0, 7)
            sp.dma_start(s_t[:, :, :], sret[0]).then_inc(state_in, 16)

            def head_stores(g):
                sp.wait_ge(sp_ready, g + 1)
                sp.dma_start(nret_p[g], sp_t[:, :]).then_inc(sp_out, 16)
                sp.wait_ge(s_new, 2 * g + 2)
                sp.dma_start(nret_s[g], s_t[:, :, :]).then_inc(state_out, 16)

            def v_to_dram(h):
                sp.wait_ge(taken, 6 * h + 4)
                sp.dma_start(v_dram, v_t[:, :, TP:NT]).then_inc(v_stored, 16)

            def spread_v(h):
                sp.wait_ge(v_stored, 16 * h + 16)
                sp.dma_start(v_all[:, :, :, :], v_dram.unsqueeze(0).to_broadcast([128, 128, 2, TS])).then_inc(v_spread, 16)

            v_to_dram(0)
            load(0, 8)
            spread_v(0)
            with sp.Fori(1, H) as h:
                for c in range(6):
                    if c == 2:
                        sp.wait_ge(gn_saved, h)
                        sp.wait_ge(s_scaled, h)
                        sp.dma_start(hc[:, :], headc[h]).then_inc(head_in, 16)
                    if c == 4:
                        head_stores(h - 1)
                    if c == 5:
                        sp.wait_ge(state_out, 16 * h)
                        sp.wait_ge(step_c, h)
                        sp.dma_start(s_t[:, :, :], sret[h]).then_inc(state_in, 16)
                        v_to_dram(h)
                    load(h, c + 3)
                    if c == 5:
                        spread_v(h)
            for i in range(51, 75):
                g, r = divmod(i - 51, 4)
                if g < 4 and r == 2:
                    if g >= 1:
                        sp.wait_ge(exts_old, g)
                    sp.dma_start(sp_in[:, :, :, :], spool[g]).then_inc(spool_in, 16)
                    if g == 0:
                        sp.wait_ge(step_b, H)
                    else:
                        sp.wait_ge(pool_mm, g)
                    sp.dma_start(pool_w[:, :], poolw[g]).then_inc(poolw_in, 16)
                if i == 52:
                    head_stores(H - 1)
                if r == 1 and 1 <= g <= 4:
                    sp.wait_ge(npool_ready, g)
                    sp.dma_start(npool_s[g - 1], nps_t[:, :, :, :]).then_inc(spool_out, 16)
                if i == 68:
                    sp.wait_ge(ppool_ready, 4)
                    sp.dma_start(npool_p, npp_t[:, :, :]).then_inc(ppool_out, 16)
                load(8, i - 48)
            sp.wait_ge(ylo_ready, H)
            sp.wait_ge(yalo_ready, 4)
            sp.wait_ge(state_out, 16 * H)
            sp.wait_ge(sp_out, 16 * H)
            sp.wait_ge(spool_out, 64)
            sp.wait_ge(ppool_out, 16)
            for s in range(2):
                sp.dma_start(gate_ring[:, s, :], ada1[s]).then_inc(gate_loaded[s], 16)
            with sp.Fori(0, 7) as it:
                for c in range(6):
                    load(12 + it, c + 3)
                    if c in (4, 5):
                        s = c - 4
                        sp.wait_ge(gate_used, 2 * it + s + 1)
                        sp.dma_start(gate_ring[:, s, :], ada1[2 * it + 2 + s]).then_inc(gate_loaded[s], 16)
            for c in range(6):
                load(19, c + 3)
            for i in range(123, 136):
                load(20, i - 120)
            sp.wait_ge(lo_ready, 136)
            sp.dma_start(x_late, xT).then_inc(x_again, 16)
            for q in range(len(Y_DVE)):
                if q in (2, 4):
                    sp.wait_ge(y_ready_p, q // 2)
                    k0, k1 = Y_POOL[q // 2 - 1]
                    sp.dma_start(yT[:, k0:k1, :], ya_out[:, k0:k1, :]).then_inc(y_out, 16)
                sp.wait_ge(y_ready, q + 1)
                k0, k1 = Y_DVE[q]
                sp.dma_start(yT[:, k0:k1, :], ya_out[:, k0:k1, :]).then_inc(y_out, 16)
            sp.wait_ge(y_out, 16 * (len(Y_DVE) + len(Y_POOL)))

        @block.tensor
        def _(pe):
            def ada_unit(bank, w, half):
                for k in range(8):
                    j = k % 4
                    mm = pe.matmul(bank[32 * j:32 * j + 32, 0:AW], cpad[:, 8 * half + k, :],
                                   w[:, AW * k:AW * k + AW], start=(half == 0 and k < 4),
                                   stop=(half == 1 and k >= 4), tile_position=(0, 32 * j))
                return mm

            def select(bank, kind):
                for t in range(2):
                    col = (2 * kind + t) * 16
                    mm = pe.matmul(bank[:, col:col + NC], part[:, kind, 128 * t:128 * t + 128], sel[:, :],
                                   start=True, stop=True)
                return mm

            def sum_up(out, wh, wl, hi, lo, ks, depth=KT):
                for k in ks:
                    cols = slice(128 * k, 128 * k + 128)
                    pe.matmul(out, wh[:, cols], hi[:, k, :], start=(k == 0), stop=False)
                    pe.matmul(out, wh[:, cols], lo[:, k, :], start=False, stop=False)
                    mm = pe.matmul(out, wl[:, cols], hi[:, k, :], start=False, stop=(k == depth - 1))
                return mm

            def products(c, par, hi, lo, ks, depth=KT, m=0):
                at = m * depth * 128
                return sum_up(P[par][:, 0:NT], w_hi[:, c % 3, at:UNIT], w_lo[:, c % 2, at:UNIT], hi, lo, ks, depth)

            def early_products(i, ks):
                return sum_up(EARLY_BANK[i][:, 0:NT], EARLY_HI[i], EARLY_LO[i], h_hi, h_lo, ks)

            def project(a, c, hi, lo, depth=KT, parts=1, after_ya=False, last=None):
                i = 6 * a + c
                pe.wait_ge(lo_ready, i + 1)
                first = outs(a, c, after_ya) - parts
                for m in range(parts):
                    par = (c + m) % 2 if parts == 1 else m % 2
                    if isinstance(a, int) and i == 5:
                        pe.wait_ge(taken, 2)
                    elif not isinstance(a, int) or first + m >= 2:
                        pe.wait_ge(taken, first + m - 1)
                    if last:
                        products(c, par, hi, lo, range(last[0]), depth, m)
                    else:
                        products(c, par, hi, lo, range(depth), depth, m).then_inc(proj_done, 1)
                if last:
                    pe.wait_ge(last[1], last[2])
                    for m in range(parts):
                        par = (c + m) % 2 if parts == 1 else m % 2
                        products(c, par, hi, lo, range(last[0], depth), depth, m).then_inc(proj_done, 1)

            pe.wait_ge(const_in, 64)
            pe.wait_ge(c_ready, 1)
            pe.wait_ge(const_ready, 1)

            def ada_pair(p, between=None):
                for s in range(4):
                    kind, half = divmod(s, 2)
                    if between:
                        between(s)
                    pe.wait_ge(ada_loaded[s], 16 * p + 16)
                    if half == 0 and p > 0:
                        pe.wait_ge(part_ready, 2 * p - 1 + kind)
                    ada_unit((TR, TV)[kind], ada_ring[:, s, :], half).then_inc(ada_used, 1)
                if p > 0:
                    pe.wait_ge(mod_ready, 2 * p)
                for kind in range(2):
                    pe.wait_ge(part_ready, 2 * p + 1 + kind)
                    select(SC, kind).then_inc(sel_done, 1)

            def x_between(s):
                if s == 2:
                    pe.wait_ge(x_sum, KT // 2)
                    pe.matmul(O0[:, 0:NT], ones[:, :], osum[:, :], start=True, stop=True).then_inc(x_ms, 1)

            ada_pair(0, x_between)
            ada_pair(1)
            for p in range(2, 6):
                ada_pair(p)
                pe.wait_ge(lo_ready, 2)
                pe.wait_ge(h_lo_ready, p - 1)
                for i in range(2):
                    early_products(i, range(2 * p - 4, 2 * p - 2))

            def unit2_between(s):
                if s == 2:
                    pe.wait_ge(lo_ready, 3)
                    pe.wait_ge(h_lo_ready, 6)
                    early_products(2, range(6))
                if s == 3:
                    early_products(2, range(6, 12))

            def unit3_between(s):
                if s == 2:
                    pe.wait_ge(lo_ready, 4)
                    early_products(3, range(U3_FIRST))

            ada_pair(6, unit2_between)
            for i in range(2):
                early_products(i, range(8, 12))
            pe.wait_ge(h_lo_ready, 7)
            for i in range(3):
                early_products(i, range(12, KT - 2))
            ada_pair(7, unit3_between)
            early_products(3, range(U3_FIRST, KT - 2))
            pe.wait_ge(h_lo_ready, 8)
            for i in range(4):
                early_products(i, range(KT - 2, KT)).then_inc(proj_done, 1)
            pe.wait_ge(lo_ready, 5)
            pe.wait_ge(taken, 1)
            early_products(4, range(KT)).then_inc(proj_done, 1)

            def a_step(h):
                pe.wait_ge(rotated, 2 * h + 2)
                pe.wait_ge(taken, 6 * h + 4)
                if not (isinstance(h, int) and h == 0):
                    pe.wait_ge(os_ready, 2 * h)
                q, k = qk_t[:, 0, :], qk_t[:, 1, :]
                for c in range(2):
                    pe.transpose(TR[:, 128 * c:128 * c + 128], k[:, 128 * c:128 * c + 128], ident[:, :])
                for c in range(2):
                    for t in range(2):
                        pe.transpose(TV[:, 256 * c + 128 * t:256 * c + 128 * t + 128],
                                     v_t[:, t, 128 * c:128 * c + 128], ident[:, :])
                pe.matmul(SC[:, 0:256], k[:, 0:128], q[:, 0:256], start=True, stop=True)
                pe.matmul(SC[:, 256:384], k[:, 128:256], q[:, 128:256], start=True, stop=True).then_inc(step_a, 1)

            def b_step(h):
                pe.wait_ge(vcen_ready, 2 * h + 2)
                pe.wait_ge(scm_ready, 2 * h + 2)
                if not (isinstance(h, int) and h == 0):
                    pe.wait_ge(std_ready, h)
                    pe.wait_ge(o_ready, 2 * h)
                for t, bank in enumerate((O0, O1)):
                    pe.matmul(bank[:, 0:256], v_cen[:, 0, 128 * t:128 * t + 128], scm[:, 0:256], start=True, stop=False)
                    mm = pe.matmul(bank[:, 128:256], v_cen[:, 1, 128 * t:128 * t + 128], scm[:, 256:384],
                                   start=False, stop=True)
                pe.wait_ge(kd_ready, 2 * h + 2)
                pe.wait_ge(vnat_ready, 2 * h + 2)
                if not (isinstance(h, int) and h == 0):
                    pe.wait_ge(o_samples, h)
                pe.matmul(ST[:, 0:256], kd[:, 0, :], v_nat[:, 0:256], start=True, stop=False)
                pe.matmul(ST[:, 0:256], kd[:, 1, :], v_nat[:, 256:512], start=False, stop=True).then_inc(step_b, 1)

            def c_step(g):
                pe.wait_ge(s_new, 2 * g + 2)
                pe.wait_ge(qpad_ready, g + 1)
                for b in range(TS):
                    j, i = b % 4, b // 4
                    mm = pe.matmul(SC[32 * j:32 * j + 32, 256 * i:256 * i + 256], qpad[:, b, :], s_t[:, b, :],
                                   start=True, stop=True, tile_position=(0, 32 * j))
                mm.then_inc(step_c, 1)

            def d_step(g):
                pe.wait_ge(oscen_ready, 2 * g + 2)
                pe.wait_ge(sp_ready, g + 1)
                for n in range(4):
                    mm = pe.matmul(ST[:, 4 * n:4 * n + 4], scm[:, 128 * n:128 * n + 128], ident[:, 0:128:32],
                                   start=True, stop=True)
                mm.then_inc(step_d, 1)

            def e_step(g):
                pe.wait_ge(sqlo_ready, g + 1)
                pe.matmul(O0[:, 0:NT], ones_r[:, :], osum_hi[:, :], start=True, stop=False)
                pe.matmul(O0[:, 0:NT], ones_r[:, :], osum_lo[:, :], start=False, stop=True).then_inc(step_e, 1)

            def head(h, first=False):
                for c in range(6):
                    if not (first and c < 5):
                        project(h, c, h_hi, h_lo)
                    if not first and 1 <= c < 4:
                        (c_step, d_step, e_step)[c - 1](h - 1)
                    if c == 4:
                        a_step(h)
                    if c == 5:
                        b_step(h)

            pe.wait_ge(const_ready, 3)
            head(0, first=True)
            with pe.Fori(1, H) as h:
                head(h)

            for g in range(4):
                for r in range(4):
                    project(8, 4 * g + r, h_hi, h_lo)
                    if g == 0 and r > 0:
                        (c_step, d_step, e_step)[r - 1](H - 1)
                pe.wait_ge(pooled_ready, 3 * g + 3)
                pe.wait_ge(poolw_in, 16 * g + 16)
                if g >= 1:
                    pe.wait_ge(yaf_ready, 2 * g)
                for t, bank in enumerate((O1, TR)):
                    for k in range(2):
                        mm = pe.matmul(bank[:, 0:NT], pool_w[:, 256 * k + 128 * t:256 * k + 128 * t + 128],
                                       pooled[:, k, :], start=(k == 0), stop=(k == 1))
                mm.then_inc(pool_mm, 1)

            pe.wait_ge(yalo_ready, 3)
            for u in range(8):
                project(8, 16 + u, ya_hi, ya_lo, depth=8, parts=2, last=(6, yalo_ready, 4) if u == 0 else None)

            pe.wait_ge(ylo_ready, H)
            pe.wait_ge(yaf_ready, 8)

            def merge(it, first=False):
                a = 12 + it
                for c in range(6):
                    if c % 3 < 2:
                        project(a, c, h_hi, h_lo, after_ya=True)
                    else:
                        project(a, c, yb_hi, yb_lo, after_ya=True)
                    if c in (1, 3):
                        s = (c - 1) // 2
                        pe.wait_ge(gate_loaded[s], 16 * it + 16)
                        if s == 0 and not first:
                            pe.wait_ge(gpart_ready, it)
                        ada_unit(TR, gate_ring[:, s, :], s).then_inc(gate_used, 1)
                    if c == 5:
                        pe.wait_ge(gpart_ready, it + 1)
                        if not first:
                            pe.wait_ge(gbias_ready, it)
                        select(SC, 0).then_inc(gsel_done, 1)

            merge(0, first=True)
            with pe.Fori(1, 8) as it:
                merge(it)

            pe.wait_ge(mlo_ready, KT - 1)
            for c in range(6):
                project(20, c, m_hi, m_lo, last=(KT - 1, mlo_ready, KT) if c == 0 else None)
            for c in range(6):
                project(21, c, m_hi, m_lo)
            for c in range(4):
                project(22, c, m_hi, m_lo)
            pe.wait_ge(out_acc, KT - 1)
            pe.matmul(O0[:, 0:NT], ones[:, :], sig_b[:, :], start=True, stop=False)
            pe.wait_ge(last_sq, 1)
            pe.matmul(O0[:, 0:NT], ones[:, :], m_f[:, :], start=False, stop=True).then_inc(out_ms, 1)

        @block.scalar
        def _(act):
            def split(a, c, after_ya=False):
                i = 6 * a + c
                act.wait_ge(raw_loaded[c % 3], 16 * (2 * a + c // 3) + 16)
                hi = w_hi[:, c % 3, :]
                if isinstance(a, int) and i < 5:
                    hi = EARLY_HI[i]
                    if i == 4:
                        act.wait_ge(ada_used, 29)
                elif not isinstance(a, int):
                    act.wait_ge(proj_done, outs(a, c - 3, after_ya))
                else:
                    act.wait_ge(proj_done, outs(0, i - 3))
                act.activation(hi, raw[:, c % 3, :], ACT.Copy).then_inc(hi_ready, 1)

            act.wait_ge(const_in, 64)
            act.wait_ge(c_zero, 1)
            act.activation(cpad[:, :, 0:NC], c_in[:, :, :], ACT.Silu).then_inc(c_ready, 1)
            act.wait_ge(const_ready, 2)
            act.activation(ones_r[:, :], ones[:, :], ACT.Copy).then_inc(const_ready, 1)
            act.wait_ge(x_in, 16)
            for n in range(KT // 2):
                if n >= 2:
                    act.wait_ge(x_sum, n - 1)
                act.activation((sq_t, bg_t)[n % 2][:, :, :], x_t[:, 2 * n:2 * n + 2, :], ACT.Square).then_inc(x_sq, 1)

            def ada_copy(p):
                for kind in range(2):
                    act.wait_ge(ada_used, 4 * p + 2 * kind + 2)
                    if not (isinstance(p, int) and p == 0):
                        act.wait_ge(sel_done, 2 * p - 1 + kind)
                    act.activation(part[:, kind, :], (TR, TV)[kind][:, 0:AW], ACT.Copy).then_inc(part_ready, 1)

            def split_h(p):
                act.wait_ge(hf_ready, 4 * p + 4)
                act.activation(h_hi[:, bass.ds(2 * p, 2), :], h_f[:, :, :], ACT.Copy).then_inc(h_hi_ready, 1)

            act.wait_ge(x_ms, 1)
            act.activation(rstd[:, :], O0[:, 0:NT], ACT.Sqrt, bias=eps_t[:, :], scale=1.0 / D_MODEL).then_inc(x_std, 1)
            ada_copy(0)
            split_h(0)
            split(0, 0)
            split(0, 1)
            with act.Fori(1, 6) as p:
                ada_copy(p)
                split_h(p)
            split(0, 2)
            ada_copy(6)
            split_h(6)
            split(0, 3)
            ada_copy(7)
            split(0, 4)
            split_h(7)

            def evac_qk(h, c):
                act.wait_ge(proj_done, 6 * h + c + 1)
                if not (isinstance(h, int) and 2 * h + c == 0):
                    act.wait_ge(rotated, 2 * h + c)
                bank = P[c % 2]
                act.activation(q_raw, bank[:, 0:NT], ACT.Copy)
                act.activation(work[0:64, 1, 0:NT], bank[64:128, 0:NT], ACT.Copy)
                act.activation(work[64:128, 1, 0:NT], bank[0:64, 0:NT], ACT.Copy).then_inc(taken, 1)

            def evac_v(h, t, bank):
                act.wait_ge(proj_done, 6 * h + t + 3)
                if not (isinstance(h, int) and h == 0):
                    act.wait_ge(step_a, h)
                    act.wait_ge(v_stored, 16 * h)
                act.activation(v_t[:, t, :], bank[:, 0:NT], ACT.Copy).then_inc(taken, 1)

            def evac_bg(h, t):
                act.wait_ge(proj_done, 6 * h + t + 5)
                if not (isinstance(h, int) and h == 0):
                    act.wait_ge(yf_ready, 2 * h)
                act.activation(bg_t[:, t, :], P[t][:, 0:NT], ACT.Silu).then_inc(taken, 1)

            def evac_os(g):
                act.wait_ge(step_c, g + 1)
                for i in range(2):
                    act.activation(scm[:, DV * i:DV * i + DV], SC[:, DV * i:DV * i + DV], ACT.Copy,
                                   accum_out=os_sum[:, i:i + 1]).then_inc(os_ready, 1)

            def squares_hi(g):
                act.wait_ge(sqs_ready, g + 1)
                if not (isinstance(g, int) and g == 0):
                    act.wait_ge(step_e, g)
                act.activation(osum_hi[:, :], osum[:, :], ACT.Copy).then_inc(sqhi_ready, 1)

            def square_root(g):
                act.wait_ge(step_e, g + 1)
                act.activation(rstd[:, :], O0[:, 0:NT], ACT.Sqrt, bias=eps_t[:, :], scale=1.0 / DV).then_inc(std_ready, 1)

            def y_hi(g):
                act.wait_ge(yf_ready, 2 * g + 2)
                act.activation(yb_hi[:, bass.ds(2 * g, 2), :], o_t[:, :, :], ACT.Copy).then_inc(yhi_ready, 1)

            def evac_b(h):
                act.wait_ge(step_b, h + 1)
                if not (isinstance(h, int) and h == 0):
                    act.wait_ge(ylo_ready, h)
                    act.wait_ge(sp_out, 16 * h)
                act.activation(o_t[:, 0, 0:TP], O0[:, 0:TP], ACT.Copy).then_inc(o_ready, 1)
                act.activation(o_t[:, 1, 0:TP], O1[:, 0:TP], ACT.Copy).then_inc(o_ready, 1)
                act.activation(sp_t[:, :], ST[:, 0:DV], ACT.Copy).then_inc(sp_ready, 1)

            def head(h, first=False):
                evac_qk(h, 0)
                split(h, 5 if first else 3)
                evac_qk(h, 1)
                if first:
                    evac_v(h, 0, EARLY_BANK[2])
                    evac_v(h, 1, EARLY_BANK[3])
                else:
                    evac_os(h - 1)
                    split(h, 4)
                    evac_v(h, 0, P[0])
                    split(h, 5)
                    squares_hi(h - 1)
                    evac_v(h, 1, P[1])
                split(h, 6)
                if not first:
                    square_root(h - 1)
                    split(h, 7)
                act.wait_ge(step_a, h + 1)
                if not first:
                    act.wait_ge(step_b, h)
                for t in range(2):
                    act.activation(v_nat[:, DV * t:DV * t + DV], TV[:, DV * t:DV * t + DV], ACT.Copy,
                                   accum_out=v_sum[:, t:t + 1]).then_inc(vnat_ready, 1)
                if first:
                    split(h, 7)
                else:
                    y_hi(h - 1)
                evac_bg(h, 0)
                act.wait_ge(state_in, 16 * h + 16)
                act.wait_ge(head_in, 16 * h + 16)
                act.activation(s_t[:, :, :], s_t[:, :, :], ACT.Copy, scale=hc[:, HC_GAMMA:HC_GAMMA + 1]).then_inc(s_scaled, 1)
                evac_bg(h, 1)
                evac_b(h)
                split(h, 8)

            head(0, first=True)
            with act.Fori(1, H) as h:
                head(h)

            for g in range(4):
                for t in range(2):
                    act.wait_ge(proj_done, 49 + 4 * g + t)
                    if g >= 1:
                        act.wait_ge(npool_ready, g)
                        act.wait_ge(pooled_ready, 3 * g)
                    else:
                        act.wait_ge(const_ready, 2)
                    act.activation(ext[:, t, 16:16 + TP], P[t][:, 0:TP], ACT.Copy)
                    act.activation(exts[:, t, :, 15], P[t][:, TP:NT], ACT.Copy).then_inc(taken, 1)
                    if g == 0 and t == 1:
                        evac_os(H - 1)
                    if g == 1 and t == 0:
                        square_root(H - 1)
                    split(8, 4 * g + t + 3)
                if g == 1:
                    y_hi(H - 1)
                if g >= 1:
                    act.wait_ge(yaf_ready, 2 * g)
                    act.activation(ya_hi[:, 2 * g - 2:2 * g, :], ya_f[:, :, :], ACT.Copy).then_inc(yahi_ready, 1)
                for t in range(2):
                    if g == 0 and t == 1:
                        squares_hi(H - 1)
                    act.wait_ge(proj_done, 51 + 4 * g + t)
                    if g == 0:
                        act.wait_ge(s_new, 2 * H)
                        act.wait_ge(qpad_ready, H)
                    else:
                        act.wait_ge(yaf_ready, 2 * g)
                    act.activation(sil_a[:, t, :], P[t][:, 0:NT], ACT.Silu).then_inc(taken, 1)
                    split(8, 4 * g + t + 5)
            act.wait_ge(yaf_ready, 8)
            act.activation(ya_hi[:, 6:8, :], ya_f[:, :, :], ACT.Copy).then_inc(yahi_ready, 1)

            act.wait_ge(ylo_ready, H)
            act.wait_ge(yalo_ready, 4)
            act.wait_ge(state_out, 16 * H)
            act.wait_ge(sp_out, 16 * H)
            act.wait_ge(spool_out, 64)
            act.wait_ge(ppool_out, 16)
            for u in range(8):
                for t in range(2):
                    n = 2 * u + t
                    act.wait_ge(proj_done, 65 + n)
                    act.activation(ya_out[:, n, :], P[t][:, 0:NT], ACT.Copy).then_inc(taken, 1)
                split(8, 19 + u)

            def merge_hi(n):
                act.wait_ge(mf_ready, n + 1)
                act.activation(m_hi[:, bass.ds(n, 1), :], m_f[:, :].unsqueeze(1), ACT.Copy).then_inc(mhi_ready, 1)

            def merge(it, first=False):
                a = 12 + it
                for c in range(6):
                    j, n = c % 3, 2 * it + c // 3
                    act.wait_ge(proj_done, 81 + 6 * it + c)
                    if not (first and c < 3):
                        act.wait_ge(mf_ready, n)
                    bank = P[c % 2][:, 0:NT]
                    if j == 0:
                        act.activation(sig_a[:, :], bank, ACT.Sigmoid, bias=vecs[:, bass.ds(V_BMERGE + n, 1)]).then_inc(taken, 1)
                    elif j == 1:
                        act.activation(sig_b[:, :], bank, ACT.Sigmoid, bias=vecs[:, bass.ds(V_BMERGE + 16 + n, 1)]).then_inc(taken, 1)
                    else:
                        act.activation(yb_out[:, :], bank, ACT.Copy).then_inc(taken, 1)
                    if j == 0 and not (first and c == 0):
                        merge_hi(n - 1)
                    split(a, c + 3, after_ya=True)
                    if c == 4:
                        act.wait_ge(gate_used, 2 * it + 2)
                        act.activation(part[:, 0, :], TR[:, 0:AW], ACT.Copy).then_inc(gpart_ready, 1)

            merge(0, first=True)
            with act.Fori(1, 8) as it:
                merge(it)

            merge_hi(KT - 1)
            act.activation(eps_sqrt[:, :], eps_t[:, :], ACT.Sqrt)

            def out_tile(a, n, c):
                act.wait_ge(proj_done, 129 + n)
                if isinstance(a, int) and n == KT - 1:
                    act.wait_ge(mlo_ready, KT)
                    act.activation(m_f[:, :], P[c % 2][:, 0:NT], ACT.Square).then_inc(last_sq, 1)
                act.activation(ya_out[:, bass.ds(n, 1), :], P[c % 2][:, 0:NT].unsqueeze(1), ACT.Copy).then_inc(taken, 1)
                if isinstance(a, int) and 6 * a + c + 3 >= 136:
                    return
                split(a, c + 3, after_ya=True)

            with act.Fori(0, 2) as m:
                for c in range(6):
                    out_tile(20 + m, 6 * m + c, c)
            for c in range(4):
                out_tile(22, 12 + c, c)
            act.wait_ge(out_ms, 1)
            act.activation(sig_a[:, :], O0[:, 0:NT], ACT.Sqrt, bias=eps_t[:, :], scale=1.0 / D_MODEL).then_inc(out_std, 1)

        @block.gpsimd
        def _(pool):
            def squares(g):
                pool.wait_ge(o_ready, 2 * g + 2)
                pool.wait_ge(o_samples, g + 1)
                pool.tensor_tensor(sq_t[:, :, :], o_t[:, :, :], o_t[:, :, :], ALU.mult).then_inc(sq_ready, 1)
                pool.wait_ge(sq_ready, g + 1)
                if not (isinstance(g, int) and g == 0):
                    pool.wait_ge(step_e, g)
                pool.tensor_tensor(osum[:, :], sq_t[:, 0, :], sq_t[:, 1, :], ALU.add).then_inc(sqs_ready, 1)

            def squares_lo(g):
                pool.wait_ge(sqhi_ready, g + 1)
                pool.tensor_tensor(osum_lo[:, :], osum[:, :], osum_hi[:, :].bitcast(f32), ALU.subtract).then_inc(sqlo_ready, 1)

            squares(0)
            squares_lo(0)
            with pool.Fori(1, H - 1) as g:
                squares(g)
                squares_lo(g)

            def windows(g):
                pool.wait_ge(taken, 50 + 4 * g)
                if g >= 1:
                    pool.wait_ge(pooled_ready, 3 * g)
                src, steps = ext, (1, 2, 4, 8)[:g + 1]
                for n, s in enumerate(steps):
                    dst = work[:, 2 * (n % 2):2 * (n % 2) + 2, :]
                    lo = 2 * s - 1
                    if n:
                        pool.wait_ge(win_step, sum(range(1, g + 1)) + n)
                    ins = pool.tensor_tensor(dst[:, :, lo:16 + TP], src[:, :, lo:16 + TP], src[:, :, lo - s:16 + TP - s], ALU.add)
                    ins.then_inc(win_step, 1)
                    src = dst

            windows(0)
            squares(H - 1)
            squares_lo(H - 1)
            for g in range(1, 4):
                windows(g)

            pool.wait_ge(out_rstd, 1)
            pool.wait_ge(out_gated, 2 * KT)
            pool.wait_ge(x_again, 16)
            for q, (k0, k1) in enumerate(Y_POOL):
                y = ya_out[:, k0:k1, :]
                pool.tensor_tensor(y, y, yb_out[:, :].unsqueeze(1).to_broadcast([128, k1 - k0, NT]), ALU.mult).then_inc(y_scaled_p, 1)
                pool.wait_ge(y_scaled_p, q + 1)
                pool.tensor_tensor(y, y, x_late[:, k0:k1, :], ALU.add).then_inc(y_ready_p, 1)

        @block.vector
        def _(dve):
            def split(a, c, after_ya=False):
                i = 6 * a + c
                dve.wait_ge(hi_ready, i + 1)
                hi, lo = w_hi[:, c % 3, :], w_lo[:, c % 2, :]
                if isinstance(a, int) and i < 5:
                    hi, lo = EARLY_HI[i], EARLY_LO[i]
                    if i == 4:
                        dve.wait_ge(ada_used, 30)
                elif not isinstance(a, int):
                    dve.wait_ge(proj_done, outs(a, c - 2, after_ya))
                else:
                    dve.wait_ge(proj_done, outs(0, i - 2))
                dve.tensor_tensor(lo, raw[:, c % 3, :], hi.bitcast(f32), ALU.subtract).then_inc(lo_ready, 1)

            dve.memset(cpad[:, :, :], 0.0).then_inc(c_zero, 1)
            dve.memset(eps_t[:, :], EPS)
            dve.memset(ones[:, :], 1.0).then_inc(const_ready, 1)
            dve.memset(ext[:, :, 0:16], 0.0)
            dve.memset(qpad[:, :, :], 0.0).then_inc(const_ready, 1)
            for n in range(KT // 2):
                dve.wait_ge(x_sq, n + 1)
                pair = (sq_t, bg_t)[n % 2]
                if n == 0:
                    dve.tensor_tensor(osum[:, :], pair[:, 0, :], pair[:, 1, :], ALU.add).then_inc(x_sum, 1)
                else:
                    dve.tensor_tensor(pair[:, 0, :], pair[:, 0, :], pair[:, 1, :], ALU.add).then_inc(hs_mul, 1)
                    dve.wait_ge(hs_mul, n)
                    dve.wait_ge(x_sum, n)
                    dve.tensor_tensor(osum[:, :], osum[:, :], pair[:, 0, :], ALU.add).then_inc(x_sum, 1)
            dve.wait_ge(x_std, 1)
            dve.reciprocal(rstd[:, :], rstd[:, :]).then_inc(x_rstd, 1)
            dve.wait_ge(x_rstd, 1)
            for k in range(KT):
                ins = dve.scalar_tensor_tensor(out=x_t[:, k, :], in0=x_t[:, k, :], scalar=vecs[:, V_GPRE + k:V_GPRE + k + 1],
                                               in1=rstd[:, :], op0=ALU.mult, op1=ALU.mult)
                ins.then_inc(xn_ready, 1)

            HM = KT // 2 - 1

            def make_h(p):
                first = isinstance(p, int) and p == 0
                dve.wait_ge(sel_done, 2 * p + 2)
                if not first:
                    dve.wait_ge(hf_ready, 4 * p)
                for kind, mod in enumerate((mod_scale, mod_shift)):
                    at = V_ADAB + (16 if kind == 0 else 0)
                    bias = vecs[:, bass.ds(2 * p + at, 2)].unsqueeze(2).to_broadcast([128, 2, NC])
                    got = SC[:, 32 * kind:32 * kind + 32].rearrange("p (t n) -> p t n", t=2)[:, :, 0:NC]
                    dve.scalar_tensor_tensor(out=mod[:, :, :], in0=got, scalar=1.0 - kind, in1=bias,
                                             op0=ALU.add, op1=ALU.add).then_inc(mod_ready, 1)
                dve.wait_ge(mod_ready, 2 * p + 2)
                dve.wait_ge(xn_ready, KT)
                if not first:
                    dve.wait_ge(h_lo_ready, p)
                    dve.wait_ge(h_hi_ready, p)
                for t in range(2):
                    dve.tensor_scalar(h_f[:, t, 0:TP].unsqueeze(1), x_t[:, bass.ds(2 * p + t, 1), 0:TP], mod_scale[:, t, 0:1], mod_shift[:, t, 0:1],
                                      ALU.mult, ALU.add).then_inc(hf_ready, 1)
                dve.tensor_tensor(h_f[:, :, TP:NT], x_t[:, bass.ds(2 * p, 2), TP:NT], mod_scale[:, :, 1:NC], ALU.mult).then_inc(hf_ready, 1)
                dve.wait_ge(hf_ready, 4 * p + 3)
                dve.tensor_tensor(h_f[:, :, TP:NT], h_f[:, :, TP:NT], mod_shift[:, :, 1:NC], ALU.add).then_inc(hf_ready, 1)
                dve.wait_ge(h_hi_ready, p + 1)
                dve.tensor_tensor(h_lo[:, bass.ds(2 * p, 2), :], h_f[:, :, :], h_hi[:, bass.ds(2 * p, 2), :].bitcast(f32),
                                  ALU.subtract).then_inc(h_lo_ready, 1)

            make_h(0)
            split(0, 0)
            split(0, 1)
            with dve.Fori(1, 6) as p:
                make_h(p)
            split(0, 2)
            make_h(6)
            split(0, 3)
            make_h(7)
            split(0, 4)
            dve.wait_ge(trig_in, 32)

            def rotate(h, c):
                n = 2 * h + c
                dve.wait_ge(taken, 6 * h + c + 1)
                scale = 1.0 if c == 0 else DK ** -0.5
                if not (isinstance(h, int) and h == 0):
                    dve.wait_ge(step_a, h)
                dve.scalar_tensor_tensor(out=q_cos, in0=q_raw, scalar=scale, in1=trig_t[:, 0, :],
                                         op0=ALU.mult, op1=ALU.mult).then_inc(rot_mul, 1)
                dve.scalar_tensor_tensor(out=q_swap, in0=q_swap, scalar=scale, in1=trig_t[:, 1, :],
                                         op0=ALU.mult, op1=ALU.mult).then_inc(rot_mul, 1)
                dve.wait_ge(rot_mul, 2 * n + 2)
                dve.tensor_tensor(qk_t[:, c, :], q_cos, q_swap, ALU.add).then_inc(rotated, 1)

            def pad_q(h):
                dve.wait_ge(rotated, 2 * h + 1)
                if not (isinstance(h, int) and h == 0):
                    dve.wait_ge(step_c, h)
                dve.tensor_copy(qpad[:, :, 0], qk_t[:, 0, TP:NT]).then_inc(qpad_ready, 1)

            def update_state(h, half):
                if half == 0:
                    dve.wait_ge(v_spread, 16 * h + 16)
                    dve.wait_ge(s_scaled, h + 1)
                for b in range(4 * half, 4 * half + 4):
                    state = s_t[:, b, :].rearrange("p (t n) -> p t n", t=2)
                    ins = dve.scalar_tensor_tensor(out=state, in0=v_all[:, :, :, b].rearrange("p n t -> p t n"),
                                                   scalar=qk_t[:, 1, TP + b:TP + b + 1], in1=state, op0=ALU.mult, op1=ALU.add)
                ins.then_inc(s_new, 1)

            def centre_v(h):
                dve.wait_ge(vnat_ready, 2 * h + 2)
                if not (isinstance(h, int) and h == 0):
                    dve.wait_ge(vcen_ready, 2 * h)
                dve.tensor_scalar(v_mean[:, :], v_sum[:, :], -1.0 / DV, None, ALU.mult).then_inc(vmean_ready, 1)
                dve.wait_ge(vmean_ready, h + 1)
                for c in range(2):
                    dve.tensor_scalar(v_cen[:, c, :], v_nat[:, DV * c:DV * c + DV], v_mean[:, c:c + 1], None,
                                      ALU.add).then_inc(vcen_ready, 1)

            def centre_samples(g):
                dve.wait_ge(os_ready, 2 * g + 2)
                dve.tensor_scalar(os_mean[:, :], os_sum[:, :], -1.0 / DV, None, ALU.mult).then_inc(osmean_ready, 1)
                dve.wait_ge(osmean_ready, g + 1)
                for i in range(2):
                    dve.tensor_scalar(scm[:, DV * i:DV * i + DV], scm[:, DV * i:DV * i + DV], os_mean[:, i:i + 1], None,
                                      ALU.add).then_inc(oscen_ready, 1)

            def collect(g):
                dve.wait_ge(step_d, g + 1)
                dve.wait_ge(o_ready, 2 * g + 2)
                src = ST[:, 0:16].rearrange("p (i t j) -> p t i j", i=2, t=2)
                dst = o_t[:, :, TP:NT].rearrange("p t (i j) -> p t i j", i=2)
                dve.tensor_copy(dst, src).then_inc(o_samples, 1)

            def norm(g):
                dve.wait_ge(std_ready, g + 1)
                dve.wait_ge(sqs_ready, g + 1)
                dve.reciprocal(rstd[:, :], rstd[:, :]).then_inc(rstd_ready, 1)
                dve.wait_ge(rstd_ready, g + 1)
                dve.wait_ge(taken, 6 * g + 6)
                for t in range(2):
                    dve.scalar_tensor_tensor(out=o_t[:, t, :], in0=o_t[:, t, :], scalar=gn_cur[:, t:t + 1], in1=rstd[:, :],
                                             op0=ALU.mult, op1=ALU.mult).then_inc(ynorm_ready, 1)
                dve.wait_ge(ynorm_ready, 2 * g + 2)
                for t in range(2):
                    dve.tensor_tensor(o_t[:, t, :], o_t[:, t, :], bg_t[:, t, :], ALU.mult).then_inc(yf_ready, 1)

            def y_lo(g):
                dve.wait_ge(yhi_ready, g + 1)
                dve.tensor_tensor(yb_lo[:, bass.ds(2 * g, 2), :], o_t[:, :, :], yb_hi[:, bass.ds(2 * g, 2), :].bitcast(f32),
                                  ALU.subtract).then_inc(ylo_ready, 1)

            def decay(h):
                dve.wait_ge(step_a, h + 1)
                dve.wait_ge(head_in, 16 * h + 16)
                if not (isinstance(h, int) and h == 0):
                    dve.wait_ge(step_b, h)
                    dve.wait_ge(step_d, h)
                dve.tensor_tensor(scm[:, 0:256], SC[:, 0:256], hc[:, 0:256], ALU.mult).then_inc(scm_ready, 1)
                dve.tensor_tensor(scm[:, 256:384], SC[:, 256:384], hc[:, 0:128], ALU.mult).then_inc(scm_ready, 1)
                for c in range(2):
                    dve.tensor_scalar(kd[:, c, :], TR[:, 128 * c:128 * c + 128], hc[:, HC_KD0 + c:HC_KD0 + c + 1], None,
                                      ALU.mult).then_inc(kd_ready, 1)

            def head(h, first=False):
                rotate(h, 0)
                if not first:
                    update_state(h - 1, 1)
                split(h, 5 if first else 2)
                rotate(h, 1)
                pad_q(h)
                if not first:
                    centre_samples(h - 1)
                    split(h, 3)
                    collect(h - 1)
                    split(h, 4)
                if not first:
                    split(h, 5)
                    norm(h - 1)
                decay(h)
                centre_v(h)
                if not first:
                    y_lo(h - 1)
                split(h, 6)
                dve.tensor_copy(gn_cur[:, :], hc[:, HC_GN:HC_GN + 2]).then_inc(gn_saved, 1)
                split(h, 7)
                update_state(h, 0)

            head(0, first=True)
            with dve.Fori(1, H) as h:
                head(h)

            def split_ya(g):
                dve.wait_ge(yahi_ready, g + 1)
                dve.tensor_tensor(ya_lo[:, 2 * g:2 * g + 2, :], ya_f[:, :, :], ya_hi[:, 2 * g:2 * g + 2, :].bitcast(f32),
                                  ALU.subtract).then_inc(yalo_ready, 1)

            update_state(H - 1, 1)
            for g in range(4):
                w = WINDOWS[g]
                split(8, 4 * g + 2)
                if g == 1:
                    norm(H - 1)
                dve.wait_ge(spool_in, 16 * g + 16)
                if g >= 1:
                    dve.wait_ge(npool_ready, g)
                dve.tensor_copy(exts[:, :, :, 0:15], sp_in[:, :, :, :]).then_inc(exts_old, 1)
                if g == 0:
                    centre_samples(H - 1)
                split(8, 4 * g + 3)
                if g == 0:
                    collect(H - 1)
                else:
                    split_ya(g - 1)
                if g == 1:
                    y_lo(H - 1)
                dve.wait_ge(taken, 50 + 4 * g)
                dve.wait_ge(exts_old, g + 1)
                if g == 0:
                    dve.wait_ge(step_a, H)
                else:
                    dve.wait_ge(pool_mm, g)
                    dve.wait_ge(spool_out, 16 * g)
                dve.tensor_reduce(win_s[:, :, :], exts[:, :, :, 16 - w:16], AX.X, ALU.add).then_inc(wins_ready, 1)
                dve.tensor_copy(npp_t[:, 2 * g:2 * g + 2, :], ext[:, :, 16 + TP - 15:16 + TP]).then_inc(ppool_ready, 1)
                dve.wait_ge(win_step, sum(range(1, g + 2)))
                win = work[:, 2 * (g % 2):2 * (g % 2) + 2, :]
                dve.scalar_tensor_tensor(out=pooled[:, :, 16:TP], in0=win[:, :, 32:16 + TP], scalar=1.0 / w,
                                         in1=ext[:, :, 32:16 + TP], op0=ALU.mult, op1=ALU.subtract).then_inc(pooled_ready, 1)
                count = cnt_t[:, g:g + 1, :].to_broadcast([128, 2, 16])
                dve.tensor_tensor(win[:, :, 16:32], win[:, :, 16:32], count, ALU.mult).then_inc(head_cols, 1)
                dve.wait_ge(head_cols, g + 1)
                dve.tensor_tensor(pooled[:, :, 0:16], win[:, :, 16:32], ext[:, :, 16:32], ALU.subtract).then_inc(pooled_ready, 1)
                dve.wait_ge(wins_ready, g + 1)
                dve.scalar_tensor_tensor(out=pooled[:, :, TP:NT], in0=win_s[:, :, :], scalar=1.0 / w, in1=exts[:, :, :, 15],
                                         op0=ALU.mult, op1=ALU.subtract).then_inc(pooled_ready, 1)
                dve.tensor_copy(nps_t[:, :, :, :], exts[:, :, :, 1:16]).then_inc(npool_ready, 1)
                split(8, 4 * g + 4)
                split(8, 4 * g + 5)
                dve.wait_ge(pool_mm, g + 1)
                dve.wait_ge(taken, 52 + 4 * g)
                if g >= 1:
                    dve.wait_ge(yalo_ready, g)
                for t, bank in enumerate((O1, TR)):
                    dve.scalar_tensor_tensor(out=ya_f[:, t, :], in0=bank[:, 0:NT], scalar=vecs[:, V_PSCALE + 2 * g + t:V_PSCALE + 2 * g + t + 1],
                                             in1=sil_a[:, t, :], op0=ALU.mult, op1=ALU.mult).then_inc(yaf_ready, 1)
            split_ya(3)

            for u in range(8):
                split(8, 18 + u)

            def merge_lo(n):
                dve.wait_ge(mhi_ready, n + 1)
                dve.tensor_tensor(m_lo[:, bass.ds(n, 1), :], m_f[:, :].unsqueeze(1), m_hi[:, bass.ds(n, 1), :].bitcast(f32),
                                  ALU.subtract).then_inc(mlo_ready, 1)

            def merge(it, first=False):
                a = 12 + it
                for c in range(6):
                    if c % 3 == 2:
                        n = 2 * it + c // 3
                        dve.wait_ge(taken, 81 + 6 * it + c)
                        if not (first and c == 2):
                            dve.wait_ge(mlo_ready, n)
                        dve.tensor_tensor(sig_a[:, :].unsqueeze(1), sig_a[:, :].unsqueeze(1), ya_out[:, bass.ds(n, 1), :], ALU.mult).then_inc(merge_mul, 1)
                        dve.tensor_tensor(sig_b[:, :], sig_b[:, :], yb_out[:, :], ALU.mult).then_inc(merge_mul, 1)
                        dve.wait_ge(merge_mul, 2 * n + 2)
                        dve.tensor_tensor(m_f[:, :], sig_a[:, :], sig_b[:, :], ALU.add).then_inc(mf_ready, 1)
                    split(a, c + 2, after_ya=True)
                    if c % 3 == 0 and not (first and c == 0):
                        merge_lo(2 * it + c // 3 - 1)
                dve.wait_ge(gsel_done, it + 1)
                tiles = bass.ds(2 * it, 2)
                got = SC[:, 0:32].rearrange("p (t n) -> p t n", t=2)[:, :, 0:NC]
                bias = vecs[:, bass.ds(2 * it + V_ADAB + 32, 2)].unsqueeze(2).to_broadcast([128, 2, NC])
                post = vecs[:, bass.ds(2 * it + V_GPOST, 2)].unsqueeze(2).to_broadcast([128, 2, NC])
                dve.tensor_tensor(mod_scale[:, :, :], got, bias, ALU.add).then_inc(gbias_ready, 1)
                dve.wait_ge(gbias_ready, it + 1)
                dve.tensor_tensor(gate_g[:, tiles, :], mod_scale[:, :, :], post, ALU.mult).then_inc(gate_ready, 1)

            merge(0, first=True)
            with dve.Fori(1, 8) as it:
                merge(it)
            merge_lo(KT - 1)

            def out_tile(a, n, c, first=False):
                dve.wait_ge(taken, 129 + n)
                tile = bass.ds(n, 1)
                o = ya_out[:, tile, :]
                if first:
                    dve.tensor_tensor(sig_b[:, :].unsqueeze(1), o, o, ALU.mult).then_inc(out_acc, 1)
                    dve.wait_ge(out_acc, 1)
                elif n < KT - 1:
                    dve.wait_ge(out_acc, n)
                    dve.tensor_tensor(sig_a[:, :].unsqueeze(1), o, o, ALU.mult).then_inc(out_sq, 1)
                    dve.wait_ge(out_sq, n)
                    dve.tensor_tensor(sig_b[:, :], sig_b[:, :], sig_a[:, :], ALU.add).then_inc(out_acc, 1)
                dve.tensor_tensor(ya_out[:, tile, 0:TP], ya_out[:, tile, 0:TP], gate_g[:, tile, 0:1].to_broadcast([128, 1, TP]),
                                  ALU.mult).then_inc(out_gated, 1)
                dve.tensor_tensor(ya_out[:, tile, TP:NT], ya_out[:, tile, TP:NT], gate_g[:, tile, 1:NC], ALU.mult).then_inc(out_gated, 1)
                if isinstance(a, int) and 6 * a + c + 2 >= 136:
                    return
                split(a, c + 2, after_ya=True)

            dve.wait_ge(gate_ready, 8)
            out_tile(20, 0, 0, first=True)
            for c in range(1, 6):
                out_tile(20, c, c)
            for c in range(6):
                out_tile(21, 6 + c, c)
            for c in range(4):
                out_tile(22, 12 + c, c)
            dve.wait_ge(out_std, 1)
            dve.reciprocal(yb_out[:, :], sig_a[:, :]).then_inc(out_rstd, 1)
            dve.wait_ge(out_rstd, 1)
            dve.wait_ge(out_gated, 2 * KT)
            dve.wait_ge(x_again, 16)
            for q, (k0, k1) in enumerate(Y_DVE):
                y = ya_out[:, k0:k1, :]
                dve.tensor_tensor(y, y, yb_out[:, :].unsqueeze(1).to_broadcast([128, k1 - k0, NT]), ALU.mult).then_inc(y_scaled, 1)
                dve.wait_ge(y_scaled, q + 1)
                dve.tensor_tensor(y, y, x_late[:, k0:k1, :], ALU.add).then_inc(y_ready, 1)


def constants():
    f = np.float32
    m = np.arange(128)
    head = np.zeros((H, 128, TP + 3))
    for h in range(H):
        lg = np.log1p(-(2.0 ** (-5.0 - h)))
        d = np.arange(TP)[None, :] - m[:, None]
        head[h, :, 0:TP] = np.where(d >= 0, np.exp(np.maximum(d, 0) * lg), 0.0)
        head[h, :, HC_KD0] = np.exp((TP - 1 - m) * lg)
        head[h, :, HC_KD1] = np.exp((127 - m) * lg)
        head[h, :, HC_GAMMA] = np.exp(lg)
    half = DK // 2
    inv = (10000.0 ** (-np.arange(half, dtype=f) / f(half))).astype(f)
    pos = np.concatenate([np.arange(TP), np.full(TS, PAST_LEN)]).astype(f)
    ang = (pos[None, :] * inv[:, None]).astype(f).astype(np.float64)
    cos, sin = np.cos(ang), np.sin(ang)
    trig = np.stack([np.concatenate([cos, cos]), np.concatenate([-sin, sin])], axis=1)
    sel = np.zeros((128, NC))
    for j in range(4):
        sel[32 * j + np.arange(NC), np.arange(NC)] = 1.0
    cnt = np.stack([1.0 / np.minimum(np.arange(16) + 1, w) for w in WINDOWS])
    cnt = np.broadcast_to(cnt, (128, 4, 16))
    return head.astype(f), trig.astype(f), np.eye(128, dtype=f), sel.astype(f), np.ascontiguousarray(cnt, dtype=f)


def kernel(x_prompt, x_sample, state_pool, state_ret, c_prompt, c_sample, ada_w, ada_b, g_pre, g_post,
           w_in, pool_w, pool_scale, gn_g, w_a_proj, w_b_proj, w_merge, b_merge, w_out):
    import concourse.bacc as bacc
    from concourse.bass_utils import run_bass_kernel_spmd

    A = lambda x: np.asarray(x)
    tiles = lambda v: A(v).reshape(-1, 128).T
    feat = lambda m: m.reshape(m.shape[0], -1, 128).transpose(2, 1, 0)
    block = lambda w, c: w[:, c:c + 128].reshape(-1, 128, 128).transpose(1, 0, 2).reshape(128, -1)

    win, wm, wa, wb, wo = A(w_in)[0], A(w_merge)[0], A(w_a_proj)[0], A(w_b_proj)[0], A(w_out)[0]
    units = []
    Q0, K0, V0, B0 = 2 * D_POOL, 2 * D_POOL + H * DK, 2 * D_POOL + 2 * H * DK, 2 * D_POOL + 2 * H * DK + H * DV
    for h in range(H):
        for c in (Q0 + DK * h, K0 + DK * h, V0 + DV * h, V0 + DV * h + 128, B0 + DV * h, B0 + DV * h + 128):
            units.append(block(win, c))
    for g in range(4):
        for c in (256 * g, 256 * g + 128, D_POOL + 256 * g, D_POOL + 256 * g + 128):
            units.append(block(win, c))
    for u in range(8):
        units.append(np.concatenate([block(wa, 256 * u), block(wa, 256 * u + 128)], axis=1))
    for n in range(KT):
        units += [block(wm, 128 * n), block(wm, D_MODEL + 128 * n), block(wb, 128 * n)]
    for n in range(KT):
        units.append(block(wo, 128 * n))
    stream = np.stack(units)

    aw = A(ada_w)[0]

    def ada_units(c):
        w = aw[:, c:c + AW].reshape(2, 8, 128, AW).transpose(0, 2, 1, 3).reshape(2, 128, UNIT)
        return [w[0], w[1]]
    ada0 = np.stack([u for p in range(8) for c in (D_MODEL + AW * p, AW * p) for u in ada_units(c)])
    ada1 = np.stack([u for p in range(8) for u in ada_units(2 * D_MODEL + AW * p)])

    head, trig, ident, sel, cnt = constants()
    gn = A(gn_g)[0].reshape(H, 2, 128).transpose(0, 2, 1)
    ins = {
        "stream": stream, "ada0": ada0, "ada1": ada1,
        "xT": np.concatenate([feat(A(x_prompt)[0]), feat(A(x_sample)[:, 0])], axis=2),
        "cT": np.concatenate([feat(A(c_prompt)), feat(A(c_sample))], axis=2),
        "vec": np.concatenate([tiles(A(g_pre)[0]), tiles(A(g_post)[0]), tiles(A(ada_b)[0]), tiles(A(b_merge)[0]),
                               tiles(A(pool_scale)[0])], axis=1),
        "headc": np.concatenate([head, gn], axis=2), "trig": trig, "ident_in": ident, "sel_in": sel, "cnt_in": cnt,
        "poolw": A(pool_w)[0].reshape(4, 2, 128, 256).transpose(0, 2, 1, 3).reshape(4, 128, 512),
        "spool": A(state_pool)[0].reshape(TS, POOL_BUF, 4, 2, 128).transpose(2, 4, 3, 0, 1),
        "sret": A(state_ret)[0].transpose(1, 2, 0, 3),
    }
    outputs = {"yT": (128, KT, NT), "npool_p": (128, 8, POOL_BUF), "npool_s": (4, 128, 2, TS, POOL_BUF),
               "nret_p": (H, 128, DV), "nret_s": (H, 128, TS, DV)}
    nc = bacc.Bacc("TRN2", target_bir_lowering=False, num_devices=1)
    arrays, aps = {}, {}
    for name, a in ins.items():
        arrays[name] = np.ascontiguousarray(a)
        aps[name] = nc.dram_tensor(name, a.shape, mybir.dt.from_np(a.dtype), kind="ExternalInput").ap()
    for name, shape in outputs.items():
        aps[name] = nc.dram_tensor(name, shape, mybir.dt.float32, kind="ExternalOutput").ap()
    aps["v_dram"] = nc.dram_tensor("v_dram", (128, 2, TS), mybir.dt.float32, kind="Internal").ap()
    build(nc, **aps)
    r = run_bass_kernel_spmd(nc, [arrays], core_ids=[0]).results[0]
    y = r["yT"].transpose(2, 1, 0).reshape(NT, D_MODEL)
    return (y[:TP].reshape(1, TP, D_MODEL), y[TP:].reshape(TS, 1, D_MODEL),
            r["npool_p"].transpose(2, 1, 0).reshape(1, 1, POOL_BUF, D_POOL),
            r["nret_p"].reshape(1, 1, H, DK, DV),
            r["npool_s"].transpose(3, 4, 0, 2, 1).reshape(1, TS, POOL_BUF, D_POOL),
            r["nret_s"].transpose(2, 0, 1, 3).reshape(1, TS, H, DK, DV))
```
